# Optimizing a Trainium2 kernel written in Bass

```python
import jax, jax.numpy as jnp
from jax import lax
import numpy as np

D_MODEL = 1024
BATCH = 1
SEQ = 1024
DEPTH = 1

HEAD_DIM = 64
H_GROUP = D_MODEL // 128
W_GROUP = H_GROUP * HEAD_DIM
N_GROUPS = 3
D_MIX = N_GROUPS * W_GROUP
D_IN = N_GROUPS * 4 * W_GROUP + H_GROUP
CHUNK = 64
N_LEFT_CHUNKS = 8
BAND = (N_LEFT_CHUNKS + 1) * CHUNK
REL_CLIP = 128
Q_BLOCK = 128
EPS = 1e-6

kernel_name = "hymba_style_sb_chunk_fox_hybrid"

def rmsnorm(x, g):
    xf = x.astype(jnp.float32)
    y = xf * lax.rsqrt(jnp.mean(xf * xf, axis=-1, keepdims=True) + EPS) * g.astype(jnp.float32)
    return y.astype(x.dtype)

def split_heads(t):
    b, s, _ = t.shape
    return t.reshape(b, s, H_GROUP, HEAD_DIM).transpose(0, 2, 1, 3)

def merge_heads(t):
    b, h, s, d = t.shape
    return t.transpose(0, 2, 1, 3).reshape(b, s, h * d)

def stick_breaking_attention(q, k, v):
    b, h, s, d = q.shape
    nb = s // Q_BLOCK
    scale = d ** -0.5
    qb = q.reshape(b, h, nb, Q_BLOCK, d).transpose(2, 0, 1, 3, 4)
    s_pos = jnp.arange(s)

    def block(args):
        qi, i = args
        t_pos = i * Q_BLOCK + jnp.arange(Q_BLOCK)
        z = jnp.einsum('bhqd,bhkd->bhqk', qi, k).astype(jnp.float32) * scale
        causal = s_pos[None, :] < t_pos[:, None]
        log_1m = jnp.where(causal, jax.nn.log_sigmoid(-z), 0.0)
        after = lax.cumsum(log_1m, axis=3, reverse=True) - log_1m
        w = jnp.where(causal, jnp.exp(jax.nn.log_sigmoid(z) + after), 0.0)
        return jnp.einsum('bhqk,bhkd->bhqd', w.astype(v.dtype), v)

    o = lax.map(block, (qb, jnp.arange(nb)))
    return o.transpose(1, 2, 0, 3, 4).reshape(b, h, s, d)

def chunked_relpos_attention(q, k, v, rel_bias):
    b, h, s, d = q.shape
    nc = s // CHUNK
    pad = N_LEFT_CHUNKS * CHUNK
    scale = d ** -0.5
    kp = jnp.pad(k, ((0, 0), (0, 0), (pad, 0), (0, 0)))
    vp = jnp.pad(v, ((0, 0), (0, 0), (pad, 0), (0, 0)))
    qc = q.reshape(b, h, nc, CHUNK, d).transpose(2, 0, 1, 3, 4)
    i_pos = jnp.arange(CHUNK)
    j_pos = jnp.arange(BAND)
    rel = i_pos[:, None] - j_pos[None, :] + pad
    bias = rel_bias[:, jnp.clip(rel, -REL_CLIP, REL_CLIP) + REL_CLIP].astype(jnp.float32)

    def block(args):
        qi, n = args
        kb = lax.dynamic_slice_in_dim(kp, n * CHUNK, BAND, axis=2)
        vb = lax.dynamic_slice_in_dim(vp, n * CHUNK, BAND, axis=2)
        z = jnp.einsum('bhqd,bhkd->bhqk', qi, kb).astype(jnp.float32) * scale + bias
        valid = (n * CHUNK - pad + j_pos) >= 0
        p = jax.nn.softmax(jnp.where(valid, z, -jnp.inf), axis=-1)
        return jnp.einsum('bhqk,bhkd->bhqd', p.astype(vb.dtype), vb)

    o = lax.map(block, (qc, jnp.arange(nc)))
    return o.transpose(1, 2, 0, 3, 4).reshape(b, h, s, d)

def forgetting_attention(q, k, v, log_f):
    b, h, s, d = q.shape
    nb = s // Q_BLOCK
    scale = d ** -0.5
    cum = lax.cumsum(log_f, axis=2)
    qb = q.reshape(b, h, nb, Q_BLOCK, d).transpose(2, 0, 1, 3, 4)
    cb = cum.reshape(b, h, nb, Q_BLOCK).transpose(2, 0, 1, 3)
    s_pos = jnp.arange(s)

    def block(args):
        qi, ci, i = args
        t_pos = i * Q_BLOCK + jnp.arange(Q_BLOCK)
        z = (jnp.einsum('bhqd,bhkd->bhqk', qi, k).astype(jnp.float32) * scale
             + ci[..., :, None] - cum[..., None, :])
        causal = s_pos[None, :] <= t_pos[:, None]
        p = jax.nn.softmax(jnp.where(causal, z, -jnp.inf), axis=-1)
        return jnp.einsum('bhqk,bhkd->bhqd', p.astype(v.dtype), v)

    o = lax.map(block, (qb, cb, jnp.arange(nb)))
    return o.transpose(1, 2, 0, 3, 4).reshape(b, h, s, d)

def hybrid_layer(x, norm_g, w_in, b_forget, q_norm_ch, k_norm_ch, q_norm_fox, k_norm_fox, rel_bias, w_out):
    h = rmsnorm(x, norm_g)
    proj = jnp.einsum('bsd,dp->bsp', h, w_in)
    split_points = [W_GROUP * (i + 1) for i in range(N_GROUPS * 4)]
    (q_sb, k_sb, v_sb, g_sb,
     q_ch, k_ch, v_ch, g_ch,
     q_fx, k_fx, v_fx, g_fx,
     f_logit) = jnp.split(proj, split_points, axis=-1)

    o_sb = stick_breaking_attention(split_heads(q_sb), split_heads(k_sb), split_heads(v_sb))

    o_ch = chunked_relpos_attention(rmsnorm(split_heads(q_ch), q_norm_ch),
                                    rmsnorm(split_heads(k_ch), k_norm_ch),
                                    split_heads(v_ch), rel_bias)

    log_f = jax.nn.log_sigmoid(f_logit.astype(jnp.float32) + b_forget.astype(jnp.float32))
    o_fx = forgetting_attention(rmsnorm(split_heads(q_fx), q_norm_fox),
                                rmsnorm(split_heads(k_fx), k_norm_fox),
                                split_heads(v_fx), log_f.transpose(0, 2, 1))

    mixed = jnp.concatenate([merge_heads(o_sb) * jax.nn.silu(g_sb),
                             merge_heads(o_ch) * jax.nn.silu(g_ch),
                             merge_heads(o_fx) * jax.nn.silu(g_fx)], axis=-1)
    return x + jnp.einsum('bsm,md->bsd', mixed, w_out)

def setup_inputs(seed: int = 0) -> dict:
    key = jax.random.key(seed)
    ks = jax.random.split(key, 10)
    f32 = jnp.float32
    x = jax.random.normal(ks[0], (BATCH, SEQ, D_MODEL), f32)
    norm_g = 1.0 + 0.02 * jax.random.normal(ks[1], (DEPTH, D_MODEL), f32)
    w_in = jax.random.normal(ks[2], (DEPTH, D_MODEL, D_IN), f32) * D_MODEL ** -0.5
    b_forget = 3.0 + 0.5 * jax.random.normal(ks[3], (DEPTH, H_GROUP), f32)
    q_norm_ch = 1.0 + 0.02 * jax.random.normal(ks[4], (DEPTH, HEAD_DIM), f32)
    k_norm_ch = 1.0 + 0.02 * jax.random.normal(ks[5], (DEPTH, HEAD_DIM), f32)
    q_norm_fox = 1.0 + 0.02 * jax.random.normal(ks[6], (DEPTH, HEAD_DIM), f32)
    k_norm_fox = 1.0 + 0.02 * jax.random.normal(ks[7], (DEPTH, HEAD_DIM), f32)
    rel_bias = 0.5 * jax.random.normal(ks[8], (DEPTH, H_GROUP, 2 * REL_CLIP + 1), f32)
    w_out = jax.random.normal(ks[9], (DEPTH, D_MIX, D_MODEL), f32) * D_MIX ** -0.5
    return {"x": x, "norm_g": norm_g, "w_in": w_in, "b_forget": b_forget,
            "q_norm_ch": q_norm_ch, "k_norm_ch": k_norm_ch,
            "q_norm_fox": q_norm_fox, "k_norm_fox": k_norm_fox,
            "rel_bias": rel_bias, "w_out": w_out}

def reference(x, norm_g, w_in, b_forget, q_norm_ch, k_norm_ch, q_norm_fox, k_norm_fox, rel_bias, w_out):
    for l in range(DEPTH):
        x = hybrid_layer(x, norm_g[l], w_in[l], b_forget[l], q_norm_ch[l], k_norm_ch[l],
                         q_norm_fox[l], k_norm_fox[l], rel_bias[l], w_out[l])
    return x


_drawn_inputs = setup_inputs


def setup_inputs(seed=0):
    import zlib

    import numpy as np

    out = dict(_drawn_inputs(seed))
    spreads = {}
    factors = {'norm_g': 6.671,
     'q_norm_ch': 8.0,
     'k_norm_ch': 8.0,
     'q_norm_fox': 8.0,
     'k_norm_fox': 8.0,
     'rel_bias': 3.834}
    for name, (base, spread) in spreads.items():
        noise = np.random.default_rng([zlib.crc32(name.encode()), seed]).standard_normal(out[name].shape)
        drawn = base * np.exp(spread * noise) if base else spread * noise
        out[name] = __import__('jax').numpy.asarray(drawn.astype(out[name].dtype))
    for name, factor in factors.items():
        out[name] = (out[name] * factor).astype(out[name].dtype)
    return out
```

```python
from contextlib import ExitStack

import numpy as np
import concourse.bass as bass
from concourse import mybir

F32 = mybir.dt.float32
F32R = mybir.dt.float32r
ALU = mybir.AluOpType
ACT = mybir.ActivationFunctionType
AX = mybir.AxisListType

P = 128
SEQ = 1024
DM = 1024
HD = 64
HG = 8
WG = HG * HD
NGROUP = 3
DMIX = NGROUP * WG
RELW = 257
CHUNK = 64
WIN = 5
EPS = 1e-6
BIG_NEG = -1e30

KT = DM // P
TT = SEQ // P
MT = DMIX // P
PAIRS = NGROUP * HG // 2
PPG = HG // 2
NB = PAIRS * 2 * TT
HALF = 512
RING = 3
REVW = P * WIN + P


def group(n):
    return n // (2 * TT * PPG)


def slot(n):
    return (n // TT) % 2


def window(n):
    b = n % TT
    return (max(0, b - WIN + 1), min(b + 1, WIN)) if group(n) == 1 else (0, b + 1)


def score_parts(n):
    k0, nb = window(n)
    w = nb * P
    if w <= HALF:
        return 0, [(0, k0 * P, max(w, 256))]
    off = 256 if w == 640 else 0
    return off, [(off, k0 * P, HALF - off), (HALF, k0 * P + HALF - off, w + off - HALF)]


def chunks(n):
    nb = window(n)[1]
    return [(c, min(4, nb - c)) for c in range(0, nb, 4)]


CHUNK0 = [0]
for _n in range(NB):
    CHUNK0.append(CHUNK0[-1] + len(chunks(_n)))


def plan():
    steps = [("x", t) for t in range(TT)] + [("forget", 0)]
    steps += [("weights", 0, k) for k in range(KT)] + [("project", 0, t) for t in range(TT)]
    steps += [("heads", 0, 0)]
    steps += [("weights", 1, k) for k in range(KT)]
    for n in range(NB + 3):
        j, r = divmod(n, 2 * TT)
        if n < NB:
            steps.append(("scores", n))
        if 2 <= n < NB + 2:
            steps.append(("values", n - 2))
        if 1 <= n < NB + 1:
            steps.append(("turn", n - 1))
        if n >= 3:
            steps.append(("fold", n - 3))
        if n >= NB:
            continue
        if r == 2:
            steps.append(("heads", j, 1))
        if 3 <= r < 3 + TT and j + 1 < PAIRS:
            steps.append(("project", j + 1, r - 3))
        if r == 11 and j + 1 < PAIRS and (j + 1) // PPG > 0:
            steps.append(("stats", j + 1))
        if r == 12 and j + 1 < PAIRS:
            steps.append(("heads", j + 1, 0))
        if r >= 12 and j + 2 < PAIRS:
            steps += [("weights", j + 2, k) for k in (2 * (r - 12), 2 * (r - 12) + 1)]
        if 3 <= r < 3 + MT and j + 1 == PAIRS:
            steps += [("wout", 0, r - 3)]
    steps.append(("mixed", 0))
    for t in range(TT):
        if t + 1 < TT:
            steps.append(("mixed", t + 1))
        steps.append(("out", t))
    return steps


PLAN = plan()


def turns_of(step):
    if step[0] in ("x", "heads"):
        return 2
    if step[0] == "turn":
        return len(chunks(step[1]))
    if step[0] == "fold":
        return 1
    if step[0] == "mixed":
        return MT // 4
    return 0


TURN0, HI0 = {}, {}
_t = _h = 0
for _s in PLAN:
    TURN0[_s], HI0[_s] = _t, _h
    _t += turns_of(_s)
    _h += turns_of(_s) if _s[0] != "fold" else 0


def wchunk(step):
    if step[0] == "weights":
        return step[1] * KT + step[2]
    return PAIRS * KT + 2 * step[2]


def build(nc, x, norm_g, w_in, b_forget, q_norm_ch, k_norm_ch, q_norm_fox, k_norm_fox, rel_bias, w_out, out):
    decay_d = nc.dram_tensor("decay_scratch", (HG, SEQ), F32).ap()
    rev_d = nc.dram_tensor("bias_scratch", (HG, REVW), F32).ap()
    skew_d = nc.dram_tensor("skew_scratch", (HG, P, REVW), F32).ap()
    mix_d = nc.dram_tensor("mixed_scratch", (SEQ, DMIX), F32).ap()

    with ExitStack() as ctx:
        def sb(name, shape, dt=F32):
            return ctx.enter_context(nc.sbuf_tensor(name, shape, dt))

        def sem(name):
            return ctx.enter_context(nc.semaphore(name))

        big = sb("big", [P, 2 * MT * DM], F32R)
        hT = [big[:, i * KT * SEQ:(i + 1) * KT * SEQ].rearrange("p (k s) -> p k s", k=KT) for i in range(2)]
        w0 = 2 * KT * SEQ
        wpair = [big[:, w0 + i * KT * HALF:w0 + (i + 1) * KT * HALF].rearrange("p (k c) -> p k c", k=KT)
                 for i in range(2)]
        wo = [big[:, i * MT * DM:(i + 1) * MT * DM].rearrange("p (k c) -> p k c", k=MT) for i in range(2)]
        wraw = sb("wraw", [P, 3, HALF])
        raw = sb("raw", [P, TT, HALF])
        stack = sb("stack", [P, 2, 3, SEQ], F32R)
        vst = sb("vst", [P, 2, TT, P], F32R)
        qks = sb("qks", [P, 2, TT, 2, HD])
        gate = sb("gate", [P, 2, TT, HD])
        zbuf = sb("zbuf", [P, 2, SEQ])
        rbuf = sb("rbuf", [P, 2, SEQ + 1])
        bias = sb("bias", [P, 2, SEQ])
        pt = sb("pt", [P, RING, 4, 2, P], F32R)
        mo = sb("mo", [P, 2, TT, HD])
        ident = sb("ident", [P, P])
        identr = sb("identr", [P, P], F32R)
        foldm = sb("foldm", [P, HD])
        mask = sb("mask", [P, 386], F32R)
        ocopy = sb("ocopy", [P, P])
        osum = sb("osum", [P, 2, P])
        gx = sb("gx", [P, KT])
        gain = sb("gain", [P, NGROUP])
        small = sb("small", [P, 4, 4])
        xs = sb("xs", [P, 2, 2])
        ms = sb("ms", [P, 32])
        rs = sb("rs", [P, 32])
        mhalf = sb("mhalf", [P, 32])
        bf = sb("bf", [HG, 1])

        psS = ctx.enter_context(nc.psum_tensor("psS", [P, 2, 2 * HALF], F32))
        psT = ctx.enter_context(nc.psum_tensor("psT", [P, 2, HALF], F32))
        psO = ctx.enter_context(nc.psum_tensor("psO", [P, HALF], F32))
        psP = ctx.enter_context(nc.psum_tensor("psP", [P, HALF], F32))

        mixin = raw[:, :, :].rearrange("p a b -> p (a b)")
        mixT = [[stack[:, i, :, :].rearrange("p a b -> p (a b)")[:, q * DMIX:(q + 1) * DMIX] for q in range(2)]
                for i in range(2)]

        s_const = sem("s_const")
        s_gain = sem("s_gain")
        s_x = [sem("s_x0"), sem("s_x1")]
        s_xsq = sem("s_xsq")
        s_ms = sem("s_ms")
        s_rs = sem("s_rs")
        s_xn = sem("s_xn")
        s_wld = [sem(f"s_wld{i}") for i in range(3)]
        s_whi = sem("s_whi")
        s_wlo = sem("s_wlo")
        s_turn = sem("s_turn")
        s_hi = sem("s_hi")
        s_evac = sem("s_evac")
        s_proj = sem("s_proj")
        s_raw = sem("s_raw")
        s_sq = sem("s_sq")
        s_sum = sem("s_sum")
        s_ss = sem("s_ss")
        s_qn = sem("s_qn")
        s_vhi = sem("s_vhi")
        s_vlo = sem("s_vlo")
        s_ge = sem("s_ge")
        s_gr = sem("s_gr")
        s_gate = sem("s_gate")
        s_scores = sem("s_scores")
        s_sig = sem("s_sig")
        s_rem = sem("s_rem")
        s_w = sem("s_w")
        s_z = sem("s_z")
        s_nm = sem("s_nm")
        s_exp = sem("s_exp")
        s_pv = sem("s_pv")
        s_oc = sem("s_oc")
        s_os = sem("s_os")
        s_rd = sem("s_rd")
        s_mo = [sem("s_mo0"), sem("s_mo1")]
        s_bias = [sem("s_bias0"), sem("s_bias1")]
        s_corner = sem("s_corner")
        s_f = sem("s_f")
        s_fd = sem("s_fd")
        s_fa = sem("s_fa")
        s_sp = sem("s_sp")
        s_wf = sem("s_wf")
        s_scr = sem("s_scr")
        s_skew = sem("s_skew")
        s_rev = sem("s_rev")
        s_revd = sem("s_revd")
        s_out = sem("s_out")
        s_mx = [sem("s_mx0"), sem("s_mx1")]
        s_oacc = sem("s_oacc")
        s_res = sem("s_res")
        s_xr = [sem("s_xr0"), sem("s_xr1")]

        wf_raw = mo[:, 0, 0, :].rearrange("p (k c) -> p k c", k=KT)
        wf_hl = [pt[:, 0, i, 0, 0:KT * HG].rearrange("p (k c) -> p k c", k=KT) for i in range(2)]
        f_rows = [bias[0:HG, 0, :], bias[0:HG, 1, :], rbuf[0:HG, 0, 0:SEQ], rbuf[0:HG, 1, 0:SEQ]]
        rel_row = wraw[0:HG, 0, 0:RELW]
        rev_row = raw[0:HG, 0:2, :].rearrange("p a b -> p (a b)")[:, 0:REVW]

        def by_head(w):
            return w.rearrange("p (h f c) -> p f h c", h=2, f=4)

        def part(f, s):
            return raw[:, :, (4 * s + f) * HD:(4 * s + f + 1) * HD]

        def nslot(n):
            a = 2 * TT * PPG
            return min(n, a), max(0, n - a)

        def last_turn(step):
            return TURN0[step] + turns_of(step)

        def bias_loads(n):
            return n // (2 * TT) - PPG + 1

        block = ctx.enter_context(nc.Block())

        @block.sync
        def _(sp):
            with nc.allow_non_contiguous_dma(reason="a few thousand single elements, once"):
                sp.dma_start(gx[:, :], norm_g[0].rearrange("(k p) -> p k", p=P)).then_inc(s_gain, 16)
                for t in range(2):
                    sp.dma_start(zbuf[:, t, :], x[0, t * P:(t + 1) * P, :]).then_inc(s_x[t], 16)
                for t, (q, k) in enumerate(((q_norm_ch, k_norm_ch), (q_norm_fox, k_norm_fox))):
                    sp.dma_start(gain[0:HD, t + 1:t + 2], q.rearrange("a d -> d a")).then_inc(s_gain, 16)
                    sp.dma_start(gain[HD:P, t + 1:t + 2], k.rearrange("a d -> d a")).then_inc(s_gain, 16)
                sp.dma_start(bf[:, :], b_forget.rearrange("a h -> h a")).then_inc(s_gain, 16)
            sp.dma_start(wf_raw, w_in[0, :, NGROUP * 4 * WG:].rearrange("(k p) c -> p k c", p=P)).then_inc(s_wf, 16)
            sp.dma_start(rel_row, rel_bias[0]).then_inc(s_rev, 16)

            def load_weights(c):
                if c < PAIRS * KT:
                    j, k = divmod(c, KT)
                    g, jj = divmod(j, PPG)
                    src = w_in[0, k * P:(k + 1) * P, g * 4 * WG:(g + 1) * 4 * WG].rearrange(
                        "p (f c) -> p f c", f=4)[:, :, jj * P:(jj + 1) * P]
                    dst = wraw[:, c % 3, :].rearrange("p (f c) -> p f c", f=4)
                elif c < PAIRS * KT + 2 * MT:
                    k, i = divmod(c - PAIRS * KT, 2)
                    src = w_out[0, k * P:(k + 1) * P, i * HALF:(i + 1) * HALF]
                    dst = wraw[:, c % 3, :]
                else:
                    return
                if c == 0:
                    sp.wait_ge(s_revd, 2)
                if c >= 3:
                    sp.wait_ge(s_wlo, c - 2)
                sp.dma_start(dst, src).then_inc(s_wld[c % 3], 16)

            for step in PLAN:
                if step[0] == "x" and step[1] + 2 < TT:
                    t = step[1] + 2
                    sp.wait_ge(s_turn, 2 * (t - 1))
                    sp.dma_start(zbuf[:, t % 2, :], x[0, t * P:(t + 1) * P, :]).then_inc(s_x[t % 2], 16)
                if step[0] == "x" and step[1] == TT - 1:
                    sp.wait_ge(s_revd, 2)
                    sp.dma_start(rev_d, rev_row).then_inc(s_scr, 16)
                    for c in range(3):
                        load_weights(c)
                if step[0] == "forget":
                    sp.wait_ge(s_scr, 16)
                    for h in range(HG):
                        sp.dma_start(skew_d[h], rev_d[h:h + 1, :].broadcast_to([P, REVW])).then_inc(s_skew, 16)
                    sp.wait_ge(s_fd, 4)
                    sp.dma_start(decay_d, f_rows[0]).then_inc(s_scr, 16)
                if step[0] in ("weights", "wout"):
                    for i in range(1 if step[0] == "weights" else 2):
                        load_weights(wchunk(step) + i + 3)
                if step[0] == "heads" and step[1] >= PPG:
                    _, j, s = step
                    if j == PPG and s == 0:
                        sp.wait_ge(s_skew, 16 * HG)
                        sp.wait_ge(s_scr, 32)
                    if j > PPG:
                        sp.wait_ge(s_z, nslot((j - 1) * 2 * TT + (s + 1) * TT)[1])
                    head = 2 * (j % PPG) + s
                    if j // PPG == 1:
                        src = bass.AP(skew_d[head].tensor, head * P * REVW + P - 1, [[REVW - 1, P], [1, P * WIN]])
                        sp.dma_start(bias[:, s, 0:P * WIN], src).then_inc(s_bias[s], 16)
                    else:
                        sp.dma_start(bias[:, s, :], decay_d[head:head + 1, :].broadcast_to([P, SEQ])
                                     ).then_inc(s_bias[s], 16)
                if step[0] == "fold" and step[1] % TT == TT - 1:
                    n = step[1]
                    h = n // TT
                    sp.wait_ge(s_evac, last_turn(step))
                    sp.dma_start(mix_d[:, h * HD:(h + 1) * HD].rearrange("(t p) c -> p t c", p=P),
                                 mo[:, slot(n), :, :]).then_inc(s_mo[slot(n)], 16)
                if step[0] == "mixed":
                    t = step[1]
                    if t == 0:
                        sp.wait_ge(s_mo[0], 16 * PAIRS)
                        sp.wait_ge(s_mo[1], 16 * PAIRS)
                    if t >= 2:
                        sp.wait_ge(s_turn, last_turn(("mixed", t - 2)))
                        sp.wait_ge(s_out, 16 * (t - 1))
                    sp.dma_start(mixin[:, (t % 2) * DMIX:(t % 2 + 1) * DMIX],
                                 mix_d[t * P:(t + 1) * P, :]).then_inc(s_mx[t % 2], 16)
                    sp.dma_start(zbuf[:, t % 2, :], x[0, t * P:(t + 1) * P, :]).then_inc(s_xr[t % 2], 16)
                if step[0] == "out":
                    t = step[1]
                    sp.wait_ge(s_res, t + 1)
                    sp.dma_start(out[0, t * P:(t + 1) * P, :], zbuf[:, t % 2, :]).then_inc(s_out, 16)
            sp.wait_ge(s_out, 16 * TT)

        @block.gpsimd
        def _(pool):
            nc.gpsimd.memset(ident[:, :], 0.0).then_inc(s_const, 1)
            nc.gpsimd.memset(foldm[:, :], 0.0).then_inc(s_const, 1)
            nc.gpsimd.memset(bias[:, 0, 0:386], 0.0).then_inc(s_const, 1)
            nc.gpsimd.memset(mhalf[:, :], -0.5).then_inc(s_const, 1)
            nc.gpsimd.memset(rbuf[:, :, SEQ:SEQ + 1], 1.0).then_inc(s_const, 1)
            pool.wait_ge(s_const, 5)
            nc.gpsimd.affine_select(out=ident[:, :], in_=ident[:, :], compare_op=ALU.not_equal, fill=1.0,
                                    base=0, pattern=[[-1, P]], channel_multiplier=1).then_inc(s_const, 1)
            nc.gpsimd.affine_select(out=foldm[:, :], in_=foldm[:, :], compare_op=ALU.not_equal, fill=1.0,
                                    base=0, pattern=[[-1, HD]], channel_multiplier=1).then_inc(s_const, 1)
            nc.gpsimd.affine_select(out=bias[:, 0, 0:386], in_=bias[:, 0, 0:386], compare_op=ALU.is_gt, fill=BIG_NEG,
                                    base=129, pattern=[[-1, 386]], channel_multiplier=1).then_inc(s_const, 1)
            pool.wait_ge(s_const, 8)
            nc.gpsimd.affine_select(out=foldm[:, :], in_=foldm[:, :], compare_op=ALU.not_equal, fill=1.0,
                                    base=-HD, pattern=[[-1, HD]], channel_multiplier=1).then_inc(s_const, 1)
            for step in PLAN:
                if step[0] == "x":
                    t = step[1]
                    pool.wait_ge(s_ms, t + 1)
                    nc.gpsimd.tensor_tensor(xs[:, t % 2, 1:2], xs[:, t % 2, 0:1], mhalf[:, 0:1],
                                            ALU.pow).then_inc(s_rs, 1)
                if step[0] == "stats":
                    pool.wait_ge(s_ss, 2 * (step[1] - PPG + 1))
                    nc.gpsimd.tensor_tensor(rs[:, :], ms[:, :], mhalf[:, :], ALU.pow).then_inc(s_rs, 1)
                if step[0] == "heads":
                    _, j, s = step
                    h = 2 * j + s
                    if j < PPG:
                        pool.wait_ge(s_ge, h + 1)
                    else:
                        pool.wait_ge(s_gr, 2 * (h - 2 * PPG) + 2)
                    nc.gpsimd.tensor_tensor(gate[:, s, :, :], gate[:, s, :, :],
                                            part(3, s), ALU.mult).then_inc(s_gate, 1)
                    if j // PPG == 1:
                        jj = j - PPG
                        pool.wait_ge(s_bias[s], 16 * (jj + 1))
                        pool.wait_ge(s_gate, h + 1)
                        nc.gpsimd.memset(bias[0:CHUNK, s, P * WIN - CHUNK:P * WIN], BIG_NEG).then_inc(s_corner, 1)
                        pool.wait_ge(s_corner, 2 * (h - 2 * PPG) + 1)
                        nc.gpsimd.memset(bias[CHUNK:P, s, 0:CHUNK], BIG_NEG).then_inc(s_corner, 1)

        @block.scalar
        def _(act):
            act.wait_ge(s_const, 9)
            nc.scalar.activation(identr[:, :], ident[:, :], ACT.Copy).then_inc(s_const, 1)
            nc.scalar.activation(mask[:, :], bias[:, 0, 0:386], ACT.Copy).then_inc(s_const, 1)
            act.wait_ge(s_gain, 6 * 16)
            act.wait_ge(s_fd, 1)
            for step in PLAN:
                kind = step[0]
                if kind == "x":
                    t = step[1]
                    act.wait_ge(s_x[t % 2], 16 * (t // 2 + 1))
                    if t:
                        act.wait_ge(s_xn, t)
                    nc.scalar.activation(rbuf[:, 0, 0:SEQ], zbuf[:, t % 2, :], ACT.Square,
                                         accum_out=xs[:, t % 2, 0:1]).then_inc(s_xsq, 1)
                    for u in range(2):
                        m = TURN0[step] + u
                        act.wait_ge(s_turn, m + 1)
                        for i in range(4):
                            k = 4 * u + i
                            ins = nc.scalar.activation(hT[0][:, k, t * P:(t + 1) * P], psT[:, m % 2, i * P:(i + 1) * P],
                                                       ACT.Copy, scale=gx[:, k:k + 1])
                        ins.then_inc(s_hi, 1)
                if kind == "forget":
                    act.wait_ge(s_wf, 16)
                    nc.scalar.activation(wf_hl[0], wf_raw, ACT.Copy).then_inc(s_fa, 1)
                    act.wait_ge(s_fd, 3)
                    nc.scalar.activation(f_rows[2], f_rows[1], ACT.Abs).then_inc(s_fa, 1)
                    act.wait_ge(s_fa, 2)
                    nc.scalar.activation(f_rows[2], f_rows[2], ACT.Exp, scale=-1.0).then_inc(s_fa, 1)
                    act.wait_ge(s_fa, 3)
                    nc.scalar.activation(f_rows[3], f_rows[2], ACT.Ln, bias=1.0).then_inc(s_fa, 1)
                if kind in ("weights", "wout"):
                    for i in range(1 if kind == "weights" else 2):
                        c = wchunk(step) + i
                        if kind == "weights":
                            dst = by_head(wpair[0][:, step[2], :])
                            src = wraw[:, c % 3, :].rearrange("p (f h c) -> p f h c", f=4, h=2)
                            if step[1] and step[2] == 0:
                                act.wait_ge(s_proj, TT * step[1])
                        else:
                            dst = wo[0][:, step[2], i * HALF:(i + 1) * HALF]
                            src = wraw[:, c % 3, :]
                            if step[2] == 0:
                                act.wait_ge(s_proj, TT * PAIRS)
                        act.wait_ge(s_wld[c % 3], 16 * (c // 3 + 1))
                        nc.scalar.activation(dst, src, ACT.Copy).then_inc(s_whi, 1)
                if kind == "project":
                    _, j, t = step
                    i = j * TT + t
                    act.wait_ge(s_proj, i + 1)
                    if t == 0 and j:
                        act.wait_ge(s_vlo, 2 * j)
                        act.wait_ge(s_gate, 2 * j)
                        if j <= PPG:
                            act.wait_ge(s_turn, last_turn(("heads", j - 1, 1)))
                        else:
                            act.wait_ge(s_qn, 2 * (j - PPG))
                    if i == 0:
                        act.wait_ge(s_scr, 16)
                    nc.scalar.activation(raw[:, t, :], psP[:, :], ACT.Copy).then_inc(s_raw, 1)
                if kind == "stats":
                    j = step[1]
                    act.wait_ge(s_raw, TT * (j + 1))
                    for s in range(2):
                        if j > PPG:
                            act.wait_ge(s_turn, last_turn(("heads", j - 1, s)))
                        nc.scalar.activation(qks[:, s, :, :, :].rearrange("p t f c -> p t (f c)"),
                                             raw[:, :, 2 * s * P:2 * s * P + P], ACT.Square).then_inc(s_sq, 1)
                if kind == "heads":
                    _, j, s = step
                    h = 2 * j + s
                    g = j // PPG
                    if j == 0:
                        act.wait_ge(s_raw, TT)
                    for u in range(2):
                        m = TURN0[step] + u
                        cols = slice(u * HALF, (u + 1) * HALF)
                        if u == 0 and j:
                            act.wait_ge(s_scores, (j - 1) * 2 * TT + (s + 1) * TT)
                        act.wait_ge(s_turn, m + 1)
                        nc.scalar.activation(stack[0:HD, s, 0, cols], psT[0:HD, m % 2, :], ACT.Copy,
                                             scale=gain[0:HD, g:g + 1])
                        nc.scalar.activation(stack[0:HD, s, 1, cols], psT[HD:P, m % 2, :], ACT.Copy,
                                             scale=gain[HD:P, g:g + 1])
                        nc.scalar.activation(stack[HD:P, s, 2, cols], psT[HD:P, m % 2, :], ACT.Copy,
                                             scale=gain[HD:P, g:g + 1]).then_inc(s_hi, 1)
                    if j:
                        act.wait_ge(s_pv, CHUNK0[(j - 1) * 2 * TT + (s + 1) * TT])
                    nc.scalar.activation(vst[:, s, :, 0:HD], part(2, s),
                                         ACT.Copy).then_inc(s_vhi, 1)
                    if j:
                        act.wait_ge(s_evac, last_turn(("fold", (j - 1) * 2 * TT + (s + 1) * TT - 1)))
                    graw = part(3, s)
                    if g == 0:
                        nc.scalar.activation(gate[:, s, :, :], graw, ACT.Sigmoid).then_inc(s_ge, 1)
                    else:
                        nc.scalar.activation(gate[:, s, :, :], graw, ACT.Exp, scale=-1.0).then_inc(s_ge, 1)
                if kind == "scores":
                    n = step[1]
                    off, _ = score_parts(n)
                    w = window(n)[1] * P
                    src = psS[:, n % 2, off:off + w]
                    q = n % 4
                    if group(n) == 0:
                        if n >= 2:
                            act.wait_ge(s_turn, last_turn(("turn", n - 2)))
                        act.wait_ge(s_scores, n + 1)
                        nc.scalar.activation(zbuf[:, n % 2, 0:w], src, ACT.Sigmoid)
                        nc.scalar.activation(rbuf[:, n % 2, 0:w], src, ACT.Sigmoid, scale=-1.0).then_inc(s_sig, 1)
                    else:
                        act.wait_ge(s_nm, nslot(n)[1] + 1)
                        if n >= 4 + 2 * TT * PPG:
                            act.wait_ge(s_rd, nslot(n)[1] - 3)
                        nc.scalar.activation(zbuf[:, n % 2, 0:w], zbuf[:, n % 2, 0:w], ACT.Exp,
                                             bias=small[:, q, 1:2], accum_out=small[:, q, 2:3]).then_inc(s_exp, 1)
                if kind == "values":
                    n = step[1]
                    act.wait_ge(s_pv, CHUNK0[n + 1])
                    nc.scalar.activation(ocopy[:, :], psO[:, 0:P], ACT.Copy).then_inc(s_oc, 1)
                if kind == "turn":
                    n = step[1]
                    for u, (c, nb) in enumerate(chunks(n)):
                        m = TURN0[step] + u
                        ci = CHUNK0[n] + u
                        if ci >= RING:
                            act.wait_ge(s_pv, ci - RING + 1)
                        act.wait_ge(s_turn, m + 1)
                        nc.scalar.activation(pt[:, ci % RING, 0:nb, 0, :],
                                             psT[:, m % 2, 0:nb * P].rearrange("p (b q) -> p b q", b=nb),
                                             ACT.Copy).then_inc(s_hi, 1)
                if kind == "mixed":
                    t = step[1]
                    if t == 0:
                        act.wait_ge(s_scores, NB)
                    if t >= 2:
                        act.wait_ge(s_oacc, t - 1)
                    for u in range(MT // 4):
                        m = TURN0[step] + u
                        act.wait_ge(s_turn, m + 1)
                        nc.scalar.activation(mixT[t % 2][0][:, u * HALF:(u + 1) * HALF], psT[:, m % 2, :],
                                             ACT.Copy).then_inc(s_hi, 1)

        @block.vector
        def _(dve):
            nc.vector.memset(gain[0:HD, 0:1], HD ** -0.5)
            nc.vector.memset(gain[HD:P, 0:1], 1.0).then_inc(s_revd, 1)
            dve.wait_ge(s_gain, 6 * 16)
            dve.wait_ge(s_revd, 1)
            nc.vector.tensor_scalar(gain[0:HD, 1:3], gain[0:HD, 1:3], HD ** -0.5, None, ALU.mult).then_inc(s_fd, 1)
            dve.wait_ge(s_rev, 16)
            nc.vector.tensor_copy(rev_row[:, 0:HALF], rel_row[:, RELW - 1:RELW].broadcast_to([HG, HALF]))
            nc.vector.tensor_copy(rev_row[:, HALF:HALF + RELW - 2], rel_row[:, RELW - 2:0:-1])
            nc.vector.memset(rev_row[:, HALF + RELW - 2:REVW], 0.0).then_inc(s_revd, 1)
            for step in PLAN:
                kind = step[0]
                if kind == "x":
                    t = step[1]
                    dve.wait_ge(s_xsq, t + 1)
                    nc.vector.tensor_scalar(xs[:, t % 2, 0:1], xs[:, t % 2, 0:1], 1.0 / DM, EPS, ALU.mult,
                                            ALU.add).then_inc(s_ms, 1)
                    dve.wait_ge(s_rs, t + 1)
                    nc.vector.tensor_scalar(zbuf[:, t % 2, :], zbuf[:, t % 2, :], xs[:, t % 2, 1:2], None,
                                            ALU.mult).then_inc(s_xn, 1)
                    for u in range(2):
                        m = TURN0[step] + u
                        dve.wait_ge(s_hi, HI0[step] + u + 1)
                        for i in range(4):
                            k = 4 * u + i
                            ins = nc.vector.scalar_tensor_tensor(
                                out=hT[1][:, k, t * P:(t + 1) * P], in0=psT[:, m % 2, i * P:(i + 1) * P],
                                scalar=gx[:, k:k + 1], in1=hT[0][:, k, t * P:(t + 1) * P].bitcast(F32),
                                op0=ALU.mult, op1=ALU.subtract)
                        ins.then_inc(s_evac, 1)
                if kind == "forget":
                    dve.wait_ge(s_fa, 1)
                    nc.vector.tensor_tensor(wf_hl[1], wf_raw, wf_hl[0].bitcast(F32), ALU.subtract).then_inc(s_fd, 1)
                    dve.wait_ge(s_f, 1)
                    nc.vector.tensor_scalar(f_rows[1], psS[0:HG, 0, :], bf[:, 0:1], -1.0, ALU.add,
                                            ALU.mult).then_inc(s_fd, 1)
                    dve.wait_ge(s_fa, 4)
                    nc.vector.scalar_tensor_tensor(out=f_rows[2], in0=f_rows[1], scalar=0.0, in1=f_rows[3],
                                                   op0=ALU.max, op1=ALU.add).then_inc(s_sp, 1)
                    dve.wait_ge(s_sp, 1)
                    nc.vector.tensor_tensor_scan(out=f_rows[0], data0=f_rows[2], data1=f_rows[2], initial=0.0,
                                                 op0=ALU.add, op1=ALU.bypass).then_inc(s_fd, 1)
                if kind in ("weights", "wout"):
                    for i in range(1 if kind == "weights" else 2):
                        c = wchunk(step) + i
                        if kind == "weights":
                            hi, lo = (by_head(w[:, step[2], :]) for w in wpair)
                            src = wraw[:, c % 3, :].rearrange("p (f h c) -> p f h c", f=4, h=2)
                        else:
                            hi, lo = (w[:, step[2], i * HALF:(i + 1) * HALF] for w in wo)
                            src = wraw[:, c % 3, :]
                        dve.wait_ge(s_whi, c + 1)
                        nc.vector.tensor_tensor(lo, src, hi.bitcast(F32), ALU.subtract).then_inc(s_wlo, 1)
                if kind == "stats":
                    j = step[1]
                    for s in range(2):
                        i = 2 * (j - PPG) + s
                        dve.wait_ge(s_sq, i + 1)
                        nc.vector.tensor_reduce(ms[:, 16 * s:16 * s + 16],
                                                qks[:, s, :, :, :].rearrange("p t f c -> p (t f) c"), AX.X,
                                                ALU.add).then_inc(s_sum, 1)
                        dve.wait_ge(s_sum, i + 1)
                        nc.vector.tensor_scalar(ms[:, 16 * s:16 * s + 16], ms[:, 16 * s:16 * s + 16], 1.0 / HD, EPS,
                                                ALU.mult, ALU.add).then_inc(s_ss, 1)
                if kind == "heads":
                    _, j, s = step
                    h = 2 * j + s
                    g = j // PPG
                    if g:
                        dve.wait_ge(s_rs, TT + j - PPG + 1)
                        for f in range(2):
                            r = rs[:, 16 * s:16 * s + 16].rearrange("p (t f) -> p t f", f=2)[:, :, f:f + 1]
                            ins = nc.vector.tensor_tensor(
                                qks[:, s, :, f, :], part(f, s),
                                r.broadcast_to([P, TT, HD]), ALU.mult)
                        ins.then_inc(s_qn, 1)
                    for u in range(2):
                        m = TURN0[step] + u
                        cols = slice(u * HALF, (u + 1) * HALF)
                        dve.wait_ge(s_hi, HI0[step] + u + 1)
                        nc.vector.scalar_tensor_tensor(
                            out=stack[HD:P, s, 0, cols], in0=psT[0:HD, m % 2, :], scalar=gain[0:HD, g:g + 1],
                            in1=stack[0:HD, s, 0, cols].bitcast(F32), op0=ALU.mult, op1=ALU.subtract)
                        nc.vector.scalar_tensor_tensor(
                            out=stack[HD:P, s, 1, cols], in0=psT[HD:P, m % 2, :], scalar=gain[HD:P, g:g + 1],
                            in1=stack[HD:P, s, 2, cols].bitcast(F32), op0=ALU.mult, op1=ALU.subtract)
                        nc.vector.scalar_tensor_tensor(
                            out=stack[0:HD, s, 2, cols], in0=psT[HD:P, m % 2, :], scalar=gain[HD:P, g:g + 1],
                            in1=stack[HD:P, s, 2, cols].bitcast(F32), op0=ALU.mult, op1=ALU.subtract
                        ).then_inc(s_evac, 1)
                    dve.wait_ge(s_vhi, h + 1)
                    nc.vector.tensor_tensor(vst[:, s, :, HD:P], part(2, s),
                                            vst[:, s, :, 0:HD].bitcast(F32), ALU.subtract).then_inc(s_vlo, 1)
                    if g:
                        i = 2 * (h - 2 * PPG)
                        dve.wait_ge(s_ge, h + 1)
                        nc.vector.tensor_scalar(gate[:, s, :, :], gate[:, s, :, :], 3.0e38, 1.0, ALU.min,
                                                ALU.add).then_inc(s_gr, 1)
                        dve.wait_ge(s_gr, i + 1)
                        nc.vector.reciprocal(gate[:, s, :, :], gate[:, s, :, :]).then_inc(s_gr, 1)
                if kind == "scores":
                    n = step[1]
                    off, _ = score_parts(n)
                    w = window(n)[1] * P
                    q = n % 4
                    if group(n) == 0:
                        dve.wait_ge(s_sig, n + 1)
                        rem = rbuf[:, n % 2, 0:w]
                        nc.vector.memset(rbuf[:, n % 2, w:w + 1], 1.0).then_inc(s_rem, 1)
                        back = rem[:, ::-1]
                        nc.vector.tensor_tensor_scan(out=back, data0=back, data1=back, initial=1.0,
                                                     op0=ALU.mult, op1=ALU.bypass).then_inc(s_rem, 1)
                        dve.wait_ge(s_rem, 2 * n + 2)
                        nc.vector.tensor_tensor(zbuf[:, n % 2, 0:w], zbuf[:, n % 2, 0:w],
                                                rbuf[:, n % 2, 1:w + 1], ALU.mult).then_inc(s_w, 1)
                    else:
                        i = nslot(n)[1]
                        if n % TT == 0:
                            dve.wait_ge(s_bias[slot(n)], 16 * bias_loads(n))
                            if group(n) == 1:
                                dve.wait_ge(s_corner, 2 * (n // TT - 2 * PPG + 1))
                        dve.wait_ge(s_turn, last_turn(("turn", n - 2)))
                        dve.wait_ge(s_scores, n + 1)
                        if i >= 4:
                            dve.wait_ge(s_exp, i - 3)
                        add = bias[:, slot(n), 0:w] if group(n) == 2 else bias[:, slot(n), P * WIN - w:P * WIN]
                        nc.vector.tensor_tensor_reduce(out=zbuf[:, n % 2, 0:w], in0=psS[:, n % 2, off:off + w],
                                                       in1=add, scale=1.0, scalar=-3.0e38, op0=ALU.add, op1=ALU.max,
                                                       accum_out=small[:, q, 0:1]).then_inc(s_z, 1)
                        dve.wait_ge(s_z, i + 1)
                        nc.vector.tensor_scalar(small[:, q, 1:2], small[:, q, 0:1], -1.0, None,
                                                ALU.mult).then_inc(s_nm, 1)
                if kind == "values":
                    n = step[1]
                    if n >= 2:
                        dve.wait_ge(s_turn, last_turn(("fold", n - 2)))
                    dve.wait_ge(s_oc, n + 1)
                    nc.vector.tensor_tensor(osum[:, n % 2, :], psO[:, P:2 * P], ocopy[:, :], ALU.add).then_inc(s_os, 1)
                if kind == "turn":
                    n = step[1]
                    for u, (c, nb) in enumerate(chunks(n)):
                        m = TURN0[step] + u
                        ci = CHUNK0[n] + u
                        dve.wait_ge(s_hi, HI0[step] + u + 1)
                        nc.vector.tensor_tensor(pt[:, ci % RING, 0:nb, 1, :],
                                                psT[:, m % 2, 0:nb * P].rearrange("p (b q) -> p b q", b=nb),
                                                pt[:, ci % RING, 0:nb, 0, :].bitcast(F32),
                                                ALU.subtract).then_inc(s_evac, 1)
                if kind == "fold":
                    n = step[1]
                    b = n % TT
                    s = slot(n)
                    m = TURN0[step]
                    if b == 0:
                        if n >= 2 * TT:
                            dve.wait_ge(s_mo[s], 16 * (n // (2 * TT)))
                        dve.wait_ge(s_gate, n // TT + 1)
                    if group(n):
                        i = nslot(n)[1]
                        dve.wait_ge(s_exp, i + 1)
                        nc.vector.reciprocal(small[:, n % 4, 3:4], small[:, n % 4, 2:3]).then_inc(s_rd, 1)
                        dve.wait_ge(s_rd, i + 1)
                    dve.wait_ge(s_turn, m + 1)
                    src = psT[:, m % 2, 0:HD]
                    if group(n):
                        nc.vector.scalar_tensor_tensor(out=mo[:, s, b, :], in0=src, scalar=small[:, n % 4, 3:4],
                                                       in1=gate[:, s, b, :], op0=ALU.mult,
                                                       op1=ALU.mult).then_inc(s_evac, 1)
                    else:
                        nc.vector.tensor_tensor(mo[:, s, b, :], src, gate[:, s, b, :], ALU.mult).then_inc(s_evac, 1)
                if kind == "mixed":
                    t = step[1]
                    for u in range(MT // 4):
                        m = TURN0[step] + u
                        dve.wait_ge(s_hi, HI0[step] + u + 1)
                        nc.vector.tensor_tensor(mixT[t % 2][1][:, u * HALF:(u + 1) * HALF], psT[:, m % 2, :],
                                                mixT[t % 2][0][:, u * HALF:(u + 1) * HALF].bitcast(F32),
                                                ALU.subtract).then_inc(s_evac, 1)
                if kind == "out":
                    t = step[1]
                    dve.wait_ge(s_oacc, t + 1)
                    dve.wait_ge(s_xr[t % 2], 16 * (t // 2 + 1))
                    nc.vector.tensor_tensor(zbuf[:, t % 2, :], psS[:, t % 2, :], zbuf[:, t % 2, :],
                                            ALU.add).then_inc(s_res, 1)

        @block.tensor
        def _(pe):
            pe.wait_ge(s_const, 11)
            for step in PLAN:
                kind = step[0]
                if kind == "x":
                    t = step[1]
                    pe.wait_ge(s_xn, t + 1)
                    for u in range(2):
                        m = TURN0[step] + u
                        if m >= 2:
                            pe.wait_ge(s_evac, m - 1)
                        for i in range(4):
                            ins = nc.tensor.transpose(psT[:, m % 2, i * P:(i + 1) * P],
                                                      zbuf[:, t % 2, (4 * u + i) * P:(4 * u + i + 1) * P], ident[:, :])
                        ins.then_inc(s_turn, 1)
                if kind == "forget":
                    pe.wait_ge(s_fd, 2)
                    pe.wait_ge(s_evac, 2 * TT)
                    for u in range(2):
                        for i, (a, b) in enumerate(((0, 0), (0, 1), (1, 0))):
                            for k in range(KT):
                                ins = nc.tensor.matmul(psS[0:HG, 0, u * HALF:(u + 1) * HALF], wf_hl[a][:, k, :],
                                                       hT[b][:, k, u * HALF:(u + 1) * HALF],
                                                       start=(i == 0 and k == 0), stop=(i == 2 and k == KT - 1))
                    ins.then_inc(s_f, 1)
                if kind == "project":
                    _, j, t = step
                    i = j * TT + t
                    if t == 0:
                        pe.wait_ge(s_wlo, KT * (j + 1))
                    if i:
                        pe.wait_ge(s_raw, i)
                    for k in range(KT):
                        for q, (a, b) in enumerate(((0, 0), (0, 1), (1, 0))):
                            ins = nc.tensor.matmul(psP[:, :], hT[a][:, k, t * P:(t + 1) * P], wpair[b][:, k, :],
                                                   start=(k == 0 and q == 0), stop=(k == KT - 1 and q == 2))
                    ins.then_inc(s_proj, 1)
                if kind == "heads":
                    _, j, s = step
                    if j < PPG:
                        pe.wait_ge(s_raw, TT * (j + 1))
                    else:
                        pe.wait_ge(s_qn, 2 * (j - PPG) + s + 1)
                    for u in range(2):
                        m = TURN0[step] + u
                        pe.wait_ge(s_evac, m - 1)
                        for i in range(4):
                            t = 4 * u + i
                            if j < PPG:
                                src = raw[:, t, 2 * s * P:2 * s * P + P]
                            else:
                                src = qks[:, s, t, :, :].rearrange("p f c -> p (f c)")
                            ins = nc.tensor.transpose(psT[:, m % 2, i * P:(i + 1) * P], src, ident[:, :])
                        ins.then_inc(s_turn, 1)
                if kind == "scores":
                    n = step[1]
                    s, b = slot(n), n % TT
                    if b == 0:
                        pe.wait_ge(s_evac, last_turn(("heads", n // (2 * TT), s)))
                    if n >= 2:
                        a, bc = nslot(n - 1)
                        if group(n - 2):
                            pe.wait_ge(s_z, bc)
                        else:
                            pe.wait_ge(s_sig, a)
                    qs = stack[:, s, 0, b * P:(b + 1) * P]
                    off, parts = score_parts(n)
                    for pi, (col, key, w) in enumerate(parts):
                        dst = psS[:, n % 2, col:col + w]
                        last = pi == len(parts) - 1
                        masked = group(n) != 1 and last
                        nc.tensor.matmul(dst, qs, stack[:, s, 1, key:key + w], start=True, stop=False)
                        ins = nc.tensor.matmul(dst, qs, stack[:, s, 2, key:key + w], start=False, stop=not masked)
                        if masked:
                            end = off + P * (b + 1) if b else 256
                            m0 = (1 if b else 1 + P) - (group(n) == 2)
                            ins = nc.tensor.matmul(psS[:, n % 2, end - 256:end], identr[:, :], mask[:, m0:m0 + 256],
                                                   start=False, stop=True)
                    ins.then_inc(s_scores, 1)
                if kind == "values":
                    n = step[1]
                    s = slot(n)
                    k0, total = window(n)
                    if n % TT == 0:
                        pe.wait_ge(s_vlo, n // TT + 1)
                    if n:
                        pe.wait_ge(s_os, n)
                    for u, (c, nb) in enumerate(chunks(n)):
                        ci = CHUNK0[n] + u
                        pe.wait_ge(s_evac, TURN0[("turn", n)] + u + 1)
                        for i in range(nb):
                            ins = nc.tensor.matmul(psO[:, 0:2 * P], vst[:, s, k0 + c + i, :],
                                                   pt[:, ci % RING, i, :, :], start=(c + i == 0),
                                                   stop=(c + i == total - 1))
                        ins.then_inc(s_pv, 1)
                if kind == "turn":
                    n = step[1]
                    a, bc = nslot(n + 1)
                    if group(n):
                        pe.wait_ge(s_exp, bc)
                    else:
                        pe.wait_ge(s_w, a)
                    for u, (c, nb) in enumerate(chunks(n)):
                        m = TURN0[step] + u
                        pe.wait_ge(s_evac, m - 1)
                        for i in range(nb):
                            ins = nc.tensor.transpose(psT[:, m % 2, i * P:(i + 1) * P],
                                                      zbuf[:, n % 2, (c + i) * P:(c + i + 1) * P], ident[:, :])
                        ins.then_inc(s_turn, 1)
                if kind == "fold":
                    n = step[1]
                    m = TURN0[step]
                    pe.wait_ge(s_os, n + 1)
                    pe.wait_ge(s_evac, m - 1)
                    nc.tensor.matmul(psT[:, m % 2, 0:HD], osum[:, n % 2, :], foldm[:, :], start=True,
                                     stop=True).then_inc(s_turn, 1)
                if kind == "mixed":
                    t = step[1]
                    pe.wait_ge(s_mx[t % 2], 16 * (t // 2 + 1))
                    for u in range(MT // 4):
                        m = TURN0[step] + u
                        pe.wait_ge(s_evac, m - 1)
                        for i in range(4):
                            c = (t % 2) * DMIX + (4 * u + i) * P
                            ins = nc.tensor.transpose(psT[:, m % 2, i * P:(i + 1) * P], mixin[:, c:c + P], ident[:, :])
                        ins.then_inc(s_turn, 1)
                if kind == "out":
                    t = step[1]
                    pe.wait_ge(s_evac, last_turn(("mixed", t)))
                    if t == 0:
                        pe.wait_ge(s_wlo, PAIRS * KT + 2 * MT)
                        pe.wait_ge(s_z, NB - 2 * TT * PPG)
                    if t >= 2:
                        pe.wait_ge(s_res, t - 1)
                    for c in range(2):
                        for k in range(MT):
                            for q, (a, b) in enumerate(((0, 0), (0, 1), (1, 0))):
                                ins = nc.tensor.matmul(psS[:, t % 2, c * HALF:(c + 1) * HALF],
                                                       mixT[t % 2][a][:, k * P:(k + 1) * P],
                                                       wo[b][:, k, c * HALF:(c + 1) * HALF],
                                                       start=(k == 0 and q == 0), stop=(k == MT - 1 and q == 2))
                    ins.then_inc(s_oacc, 1)


_INS = ["x", "norm_g", "w_in", "b_forget", "q_norm_ch", "k_norm_ch", "q_norm_fox", "k_norm_fox", "rel_bias", "w_out"]


def kernel(**inputs):
    import numpy as _np
    import concourse.bacc as _bacc
    from concourse import mybir as _mybir
    from concourse.bass_utils import run_bass_kernel_spmd as _run

    nc = _bacc.Bacc("TRN2", target_bir_lowering=False, num_devices=1)
    arrays, args = {}, []
    for name in _INS:
        a = _np.ascontiguousarray(inputs[name])
        arrays[f"in_{name}_dram"] = a
        args.append(nc.dram_tensor(f"in_{name}_dram", a.shape, _mybir.dt.from_np(a.dtype), kind="ExternalInput").ap())
    args.append(nc.dram_tensor("out_0_dram", (1, SEQ, DM), _mybir.dt.float32, kind="ExternalOutput").ap())
    build(nc, *args)
    r = _run(nc, [arrays], core_ids=[0])
    return r.results[0]["out_0_dram"]
```

```python
from contextlib import ExitStack

import numpy as np
import concourse.bass as bass
from concourse import mybir

F32 = mybir.dt.float32
F32R = mybir.dt.float32r
ALU = mybir.AluOpType
ACT = mybir.ActivationFunctionType
AX = mybir.AxisListType

P = 128
SEQ = 1024
DM = 1024
HD = 64
HG = 8
WG = HG * HD
NGROUP = 3
DMIX = NGROUP * WG
RELW = 257
CHUNK = 64
WIN = 5
EPS = 1e-6
BIG_NEG = -1e30

KT = DM // P
TT = SEQ // P
MT = DMIX // P
PAIRS = NGROUP * HG // 2
PPG = HG // 2
NB = PAIRS * 2 * TT
HALF = 512
RING = 3
REVW = P * WIN + P


def group(n):
    return n // (2 * TT * PPG)


def slot(n):
    return (n // TT) % 2


def window(n):
    b = n % TT
    return (max(0, b - WIN + 1), min(b + 1, WIN)) if group(n) == 1 else (0, b + 1)


def score_parts(n):
    k0, nb = window(n)
    w = nb * P
    if w <= HALF:
        return 0, [(0, k0 * P, max(w, 256))]
    off = 256 if w == 640 else 0
    return off, [(off, k0 * P, HALF - off), (HALF, k0 * P + HALF - off, w + off - HALF)]


def chunks(n):
    nb = window(n)[1]
    return [(c, min(4, nb - c)) for c in range(0, nb, 4)]


CHUNK0 = [0]
for _n in range(NB):
    CHUNK0.append(CHUNK0[-1] + len(chunks(_n)))


def extras(j, r):
    found = []
    if r == 0:
        if j:
            found.append([("norm", j, 1)])
        if j + 1 < PAIRS:
            found.append([("weights", j + 1, KT - 2), ("weights", j + 1, KT - 1)])
    if r == 1:
        found += [[("vgate", j, 1, 0)], [("heads", j, 0, 1)], [("vgate", j, 0, 1)]]
    if r == 3:
        found.append([("heads", j, 1, 0)])
    if r == 4:
        found.append([("vgate", j, 1, 1)])
    if r == 5:
        found.append([("heads", j, 1, 1)])
    if j + 1 < PAIRS:
        if r in (9, 15) and j + 1 >= PPG:
            found.append([("stats", j + 1, r // 15)])
        if r == 10:
            found.append([("norm", j + 1, 0)])
        if r == 11:
            found += [[("heads", j + 1, 0, 0)], [("vgate", j + 1, 0, 0)]]
    if 13 <= r and j + 2 < PAIRS:
        found.append([("weights", j + 2, k) for k in (2 * (r - 13), 2 * (r - 13) + 1)])
    if r < MT and j + 1 == PAIRS:
        found.append([("wout", 0, r)])
    return found


def plan():
    steps = [("square", 0), ("square", 1)]
    for t in range(TT):
        steps.append(("x", t))
        if t + 2 < TT:
            steps.append(("square", t + 2))
        if t < 4:
            steps += [("weights", 0, 2 * t), ("weights", 0, 2 * t + 1)]
        if t >= 4:
            steps += [("project", 0, t - 4, 0, KT), ("raw", 0, t - 4)]
    for t in range(4, TT):
        steps += [("project", 0, t, 0, KT), ("raw", 0, t)]
    steps += [("norm", 0, 0), ("norm", 0, 1), ("heads", 0, 0, 0), ("vgate", 0, 0, 0)]
    steps += [("weights", 1, k) for k in range(KT - 2)]
    steps.append(("forget", 0))
    for n in range(NB + 3):
        j, r = divmod(n, 2 * TT)
        items = []
        if n < NB:
            items.append([("scores", n)])
        if n >= 3:
            items.append([("fold", n - 3)])
        if 2 <= n < NB + 2:
            items.append([("values", n - 2)])
        if 1 <= n < NB + 1:
            items += [[("turn", n - 1, u)] for u in range(len(chunks(n - 1)))]
        if n < NB:
            items += extras(j, r)
        if r == 0:
            done = rest = 0
        for i, item in enumerate(items):
            steps += item
            if n < NB and j + 1 < PAIRS:
                t, k = divmod(done, KT)
                k1 = min(KT, k + UNIT0[r] + (i + 1) * UNITS[r] // len(items) - done)
                rest -= 1
                if k1 > k and rest < 0:
                    steps += [("project", j + 1, t, k, k1)] + ([("raw", j + 1, t)] if k1 == KT else [])
                    done += k1 - k
                    if k1 == KT:
                        rest = REST
    steps.append(("mixed", 0))
    for t in range(TT):
        if t + 1 < TT:
            steps.append(("mixed", t + 1))
        steps.append(("out", t))
    return steps


UNITS = [4, 4, 5, 5, 5, 4, 4, 3, 5, 5, 5, 4, 4, 4, 3, 0]
REST = 1
UNIT0 = [sum(UNITS[:r]) for r in range(2 * TT + 1)]
assert UNIT0[-1] == KT * TT

PLAN = plan()


def turns_of(step):
    if step[0] == "x":
        return 2
    if step[0] == "heads":
        return 1
    if step[0] == "turn":
        return 1
    if step[0] == "fold":
        return 1
    if step[0] == "mixed":
        return MT // 4
    return 0


TURN0, HI0 = {}, {}
_t = _h = 0
for _s in PLAN:
    TURN0[_s], HI0[_s] = _t, _h
    _t += turns_of(_s)
    _h += turns_of(_s) if _s[0] != "fold" else 0


VGATE = {s[1:]: i for i, s in enumerate(s for s in PLAN if s[0] == "vgate")}
NORM = {s[1:]: i for i, s in enumerate(s for s in PLAN if s[0] == "norm")}
NORM_A = 2 * PPG


def wchunk(step):
    if step[0] == "weights":
        return step[1] * KT + step[2]
    return PAIRS * KT + 2 * step[2]


def build(nc, x, norm_g, w_in, b_forget, q_norm_ch, k_norm_ch, q_norm_fox, k_norm_fox, rel_bias, w_out, out):
    decay_d = nc.dram_tensor("decay_scratch", (HG, SEQ), F32).ap()
    rev_d = nc.dram_tensor("bias_scratch", (HG, REVW), F32).ap()
    skew_d = nc.dram_tensor("skew_scratch", (HG, P, REVW), F32).ap()
    mix_d = nc.dram_tensor("mixed_scratch", (SEQ, DMIX), F32).ap()

    with ExitStack() as ctx:
        def sb(name, shape, dt=F32):
            return ctx.enter_context(nc.sbuf_tensor(name, shape, dt))

        def sem(name):
            return ctx.enter_context(nc.semaphore(name))

        big = sb("big", [P, 2 * MT * DM], F32R)
        hT = [big[:, i * KT * SEQ:(i + 1) * KT * SEQ].rearrange("p (k s) -> p k s", k=KT) for i in range(2)]
        w0 = 2 * KT * SEQ
        wpair = [big[:, w0 + i * KT * HALF:w0 + (i + 1) * KT * HALF].rearrange("p (k c) -> p k c", k=KT)
                 for i in range(2)]
        wo = [big[:, i * MT * DM:(i + 1) * MT * DM].rearrange("p (k c) -> p k c", k=MT) for i in range(2)]
        wraw = sb("wraw", [P, 3, HALF])
        raw = sb("raw", [P, TT, HALF])
        stack = sb("stack", [P, 2, 3, SEQ], F32R)
        vst = sb("vst", [P, 2, TT, P], F32R)
        qks = sb("qks", [P, 2, TT, 2, HD])
        gate = sb("gate", [P, 2, TT, HD])
        zbuf = sb("zbuf", [P, 2, SEQ])
        rbuf = sb("rbuf", [P, 2, SEQ + 1])
        bias = sb("bias", [P, 2, SEQ])
        pt = sb("pt", [P, RING, 4, 2, P], F32R)
        mo = sb("mo", [P, 2, TT, HD])
        ident = sb("ident", [P, P])
        identr = sb("identr", [P, P], F32R)
        foldm = sb("foldm", [P, HD])
        mask = sb("mask", [P, 386], F32R)
        ocopy = sb("ocopy", [P, P])
        osum = sb("osum", [P, 2, P])
        gain = sb("gain", [P, NGROUP])
        small = sb("small", [P, 4, 4])
        xs = sb("xs", [P, 2, 2])
        ms = sb("ms", [P, 32])
        rs = sb("rs", [P, 32])
        mhalf = sb("mhalf", [P, 32])
        bf = sb("bf", [HG, 1])

        psS = ctx.enter_context(nc.psum_tensor("psS", [P, 2, 2 * HALF], F32))
        psT = ctx.enter_context(nc.psum_tensor("psT", [P, 2, HALF], F32))
        psO = ctx.enter_context(nc.psum_tensor("psO", [P, HALF], F32))
        psP = ctx.enter_context(nc.psum_tensor("psP", [P, HALF], F32))

        mixin = raw[:, :, :].rearrange("p a b -> p (a b)")
        mixT = [[stack[:, i, :, :].rearrange("p a b -> p (a b)")[:, q * DMIX:(q + 1) * DMIX] for q in range(2)]
                for i in range(2)]

        s_const = sem("s_const")
        s_gain = sem("s_gain")
        s_x = [sem(f"s_x{i}") for i in range(4)]
        s_xsq = sem("s_xsq")
        s_ms = sem("s_ms")
        s_rs = sem("s_rs")
        s_xn = sem("s_xn")
        s_wld = [sem(f"s_wld{i}") for i in range(3)]
        s_whi = sem("s_whi")
        s_wlo = sem("s_wlo")
        s_turn = sem("s_turn")
        s_hi = sem("s_hi")
        s_evac = sem("s_evac")
        s_proj = sem("s_proj")
        s_wk = sem("s_wk")
        s_raw = sem("s_raw")
        s_sq = sem("s_sq")
        s_sum = sem("s_sum")
        s_ss = sem("s_ss")
        s_qc = sem("s_qc")
        s_qn = sem("s_qn")
        s_vhi = sem("s_vhi")
        s_vlo = sem("s_vlo")
        s_ge = sem("s_ge")
        s_gate = sem("s_gate")
        s_scores = sem("s_scores")
        s_sig = sem("s_sig")
        s_rem = sem("s_rem")
        s_w = sem("s_w")
        s_z = sem("s_z")
        s_nm = sem("s_nm")
        s_exp = sem("s_exp")
        s_pv = sem("s_pv")
        s_oc = sem("s_oc")
        s_os = sem("s_os")
        s_rd = sem("s_rd")
        s_mo = [sem(f"s_mo{i}") for i in range(4)]
        s_bias = [sem("s_bias0"), sem("s_bias1")]
        s_corner = sem("s_corner")
        s_f = sem("s_f")
        s_fd = sem("s_fd")
        s_fa = sem("s_fa")
        s_sp = sem("s_sp")
        s_wf = sem("s_wf")
        s_scr = sem("s_scr")
        s_skew = sem("s_skew")
        s_rev = sem("s_rev")
        s_revd = sem("s_revd")
        s_out = [sem("s_out0"), sem("s_out1")]
        s_mx = [sem("s_mx0"), sem("s_mx1")]
        s_oacc = sem("s_oacc")
        s_res = sem("s_res")
        s_xr = [sem("s_xr0"), sem("s_xr1")]

        wf_raw = ocopy[:, 0:KT * HG].rearrange("p (k c) -> p k c", k=KT)
        wf_hl = [pt[:, 0, i, 0, 0:KT * HG].rearrange("p (k c) -> p k c", k=KT) for i in range(2)]
        f_rows = [bias[0:HG, 0, :], bias[0:HG, 1, :], rbuf[0:HG, 0, 0:SEQ], rbuf[0:HG, 1, 0:SEQ]]
        rel_row = osum[0:HG, :, :].rearrange("p a b -> p (a b)")
        rev_row = mo[0:HG, :, :, :].rearrange("p a b c -> p (a b c)")[:, 0:REVW]
        gx = bias[:, 1, :]
        xt = [raw[:, 2 * i:2 * i + 2, :].rearrange("p a b -> p (a b)") for i in range(4)]

        def by_head(w):
            return w.rearrange("p (h f c) -> p f h c", h=2, f=4)

        def part(f, s, u):
            return raw[:, 4 * u:4 * u + 4, (4 * s + f) * HD:(4 * s + f + 1) * HD]

        def nslot(n):
            a = 2 * TT * PPG
            return min(n, a), max(0, n - a)

        def last_turn(step):
            return TURN0[step] + turns_of(step)

        def turned(n):
            return last_turn(("turn", n, len(chunks(n)) - 1))

        def bias_loads(n):
            return n // (2 * TT) - PPG + 1

        block = ctx.enter_context(nc.Block())

        @block.sync
        def _(sp):
            def load_mixed(t):
                if t % 4 == 0:
                    sp.wait_ge(s_mo[t // 2], 16 * PAIRS)
                    sp.wait_ge(s_mo[t // 2 + 1], 16 * PAIRS)
                if t >= 2:
                    sp.wait_ge(s_turn, last_turn(("mixed", t - 2)))
                sp.dma_start(mixin[:, (t % 2) * DMIX:(t % 2 + 1) * DMIX],
                             mix_d[t * P:(t + 1) * P, :]).then_inc(s_mx[t % 2], 16)
                if t < 2:
                    sp.wait_ge(s_turn, turned(NB - 2 + t))
                else:
                    sp.wait_ge(s_res, t - 1)
                sp.dma_start(zbuf[:, t % 2, :], x[0, t * P:(t + 1) * P, :]).then_inc(s_xr[t % 2], 16)

            def load_weights(c):
                if c < PAIRS * KT:
                    j, k = divmod(c, KT)
                    g, jj = divmod(j, PPG)
                    src = w_in[0, k * P:(k + 1) * P, g * 4 * WG:(g + 1) * 4 * WG].rearrange(
                        "p (f c) -> p f c", f=4)[:, :, jj * P:(jj + 1) * P]
                    dst = wraw[:, c % 3, :].rearrange("p (f c) -> p f c", f=4)
                elif c < PAIRS * KT + 2 * MT:
                    k, i = divmod(c - PAIRS * KT, 2)
                    src = w_out[0, k * P:(k + 1) * P, i * HALF:(i + 1) * HALF]
                    dst = wraw[:, c % 3, :]
                else:
                    return
                if c >= 3:
                    sp.wait_ge(s_wlo, c - 2)
                sp.dma_start(dst, src).then_inc(s_wld[c % 3], 16)

            sp.dma_start(xt[0], x[0, 0:P, :]).then_inc(s_x[0], 16)
            sp.dma_start(gx, norm_g[0:1, :].broadcast_to([P, DM])).then_inc(s_gain, 16)
            for t in range(1, 4):
                sp.dma_start(xt[t], x[0, t * P:(t + 1) * P, :]).then_inc(s_x[t], 16)
            for c in range(3):
                load_weights(c)
            with nc.allow_non_contiguous_dma(reason="the gains, once"):
                for t, (q, k) in enumerate(((q_norm_ch, k_norm_ch), (q_norm_fox, k_norm_fox))):
                    sp.dma_start(gain[0:HD, t + 1:t + 2], q.rearrange("a d -> d a")).then_inc(s_gain, 16)
                    sp.dma_start(gain[HD:P, t + 1:t + 2], k.rearrange("a d -> d a")).then_inc(s_gain, 16)
                sp.dma_start(bf[:, :], b_forget.rearrange("a h -> h a")).then_inc(s_gain, 16)
            sp.dma_start(wf_raw, w_in[0, :, NGROUP * 4 * WG:].rearrange("(k p) c -> p k c", p=P)).then_inc(s_wf, 16)
            sp.dma_start(rel_row, rel_bias[0, :, 1:RELW]).then_inc(s_rev, 16)

            for step in PLAN:
                if step[0] == "x" and step[1] + 4 < TT:
                    t = step[1] + 4
                    sp.wait_ge(s_turn, 2 * (t - 3))
                    sp.dma_start(xt[t % 4], x[0, t * P:(t + 1) * P, :]).then_inc(s_x[t % 4], 16)
                if step == ("x", 4):
                    sp.wait_ge(s_revd, 2)
                    sp.dma_start(rev_d, rev_row).then_inc(s_scr, 16)
                if step[0] == "forget":
                    sp.wait_ge(s_scr, 16)
                    for h in range(HG):
                        sp.dma_start(skew_d[h], rev_d[h:h + 1, :].broadcast_to([P, REVW])).then_inc(s_skew, 16)
                    sp.wait_ge(s_fd, 4)
                    sp.dma_start(decay_d, f_rows[0]).then_inc(s_scr, 16)
                if step[0] in ("weights", "wout"):
                    for i in range(1 if step[0] == "weights" else 2):
                        load_weights(wchunk(step) + i + 3)
                if step[0] == "heads" and step[1] >= PPG and step[3] == 0:
                    _, j, s, _ = step
                    if j == PPG and s == 0:
                        sp.wait_ge(s_skew, 16 * HG)
                        sp.wait_ge(s_scr, 32)
                    if j > PPG:
                        sp.wait_ge(s_z, nslot((j - 1) * 2 * TT + (s + 1) * TT)[1])
                    head = 2 * (j % PPG) + s
                    if j // PPG == 1:
                        src = bass.AP(skew_d[head].tensor, head * P * REVW + P - 1, [[REVW - 1, P], [1, P * WIN]])
                        sp.dma_start(bias[:, s, 0:P * WIN], src).then_inc(s_bias[s], 16)
                    else:
                        sp.dma_start(bias[:, s, :], decay_d[head:head + 1, :].broadcast_to([P, SEQ])
                                     ).then_inc(s_bias[s], 16)
                if step[0] == "fold" and step[1] % 4 == 3:
                    n = step[1]
                    h, u = n // TT, n % TT // 4
                    sp.wait_ge(s_evac, last_turn(step))
                    sp.dma_start(mix_d[u * HALF:(u + 1) * HALF, h * HD:(h + 1) * HD].rearrange("(t p) c -> p t c", p=P),
                                 mo[:, slot(n), 4 * u:4 * u + 4, :]).then_inc(s_mo[2 * u + slot(n)], 16)
                    if n == NB - 5:
                        for t in range(2):
                            load_mixed(t)
                if step[0] == "out":
                    t = step[1]
                    if t + 2 < TT:
                        load_mixed(t + 2)
                    sp.wait_ge(s_res, t + 1)
                    sp.dma_start(out[0, t * P:(t + 1) * P, :], rbuf[:, t % 2, 0:SEQ]).then_inc(s_out[t % 2], 16)
            for o in s_out:
                sp.wait_ge(o, 16 * (TT // 2))

        @block.gpsimd
        def _(pool):
            nc.gpsimd.memset(ident[:, :], 0.0).then_inc(s_const, 1)
            nc.gpsimd.memset(foldm[:, :], 0.0).then_inc(s_const, 1)
            nc.gpsimd.memset(bias[:, 0, 0:386], 0.0).then_inc(s_const, 1)
            nc.gpsimd.memset(mhalf[:, :], -0.5).then_inc(s_const, 1)
            nc.gpsimd.memset(rbuf[:, :, SEQ:SEQ + 1], 1.0).then_inc(s_const, 1)
            pool.wait_ge(s_const, 5)
            nc.gpsimd.affine_select(out=ident[:, :], in_=ident[:, :], compare_op=ALU.not_equal, fill=1.0,
                                    base=0, pattern=[[-1, P]], channel_multiplier=1).then_inc(s_const, 1)
            nc.gpsimd.affine_select(out=foldm[:, :], in_=foldm[:, :], compare_op=ALU.not_equal, fill=0.5,
                                    base=0, pattern=[[-1, HD]], channel_multiplier=1).then_inc(s_const, 1)
            nc.gpsimd.affine_select(out=bias[:, 0, 0:386], in_=bias[:, 0, 0:386], compare_op=ALU.is_gt, fill=BIG_NEG,
                                    base=129, pattern=[[-1, 386]], channel_multiplier=1).then_inc(s_const, 1)
            pool.wait_ge(s_const, 8)
            nc.gpsimd.affine_select(out=foldm[:, :], in_=foldm[:, :], compare_op=ALU.not_equal, fill=0.5,
                                    base=-HD, pattern=[[-1, HD]], channel_multiplier=1).then_inc(s_const, 1)
            for step in PLAN:
                if step[0] == "square":
                    t = step[1]
                    pool.wait_ge(s_ms, t + 1)
                    nc.gpsimd.tensor_tensor(xs[:, t % 2, 1:2], xs[:, t % 2, 0:1], mhalf[:, 0:1],
                                            ALU.pow).then_inc(s_rs, 1)
                if step[0] == "stats":
                    _, j, u = step
                    pool.wait_ge(s_ss, 2 * (j - PPG) + u + 1)
                    nc.gpsimd.tensor_tensor(rs[:, 16 * u:16 * u + 16], ms[:, 16 * u:16 * u + 16], mhalf[:, 0:16],
                                            ALU.pow).then_inc(s_rs, 1)
                if step[0] == "norm" and step[1] < PPG:
                    _, j, u = step
                    pool.wait_ge(s_raw, TT * j + 4 * u + 4)
                    if j:
                        pool.wait_ge(s_turn, last_turn(("heads", j - 1, 1, u)))
                    nc.gpsimd.tensor_copy(
                        qks[:, :, 4 * u:4 * u + 4, :, :].rearrange("p s t f c -> p t s (f c)"),
                        raw[:, 4 * u:4 * u + 4, :].rearrange("p t (s c) -> p t s c", s=2)[:, :, :, 0:P]).then_inc(s_qc, 1)
                    pool.wait_ge(s_qc, NORM[j, u] + 1)
                if step[0] == "vgate" and step[1] // PPG == 1 and step[3] == 0:
                    _, j, s, u = step
                    jj = j - PPG
                    pool.wait_ge(s_bias[s], 16 * (jj + 1))
                    nc.gpsimd.memset(bias[0:CHUNK, s, P * WIN - CHUNK:P * WIN], BIG_NEG).then_inc(s_corner, 1)
                    pool.wait_ge(s_corner, 2 * (2 * jj + s) + 1)
                    nc.gpsimd.memset(bias[CHUNK:P, s, 0:CHUNK], BIG_NEG).then_inc(s_corner, 1)
                    pool.wait_ge(s_corner, 2 * (2 * jj + s) + 2)

        @block.scalar
        def _(act):
            act.wait_ge(s_const, 9)
            nc.scalar.activation(identr[:, :], ident[:, :], ACT.Copy).then_inc(s_const, 1)
            nc.scalar.activation(mask[:, :], bias[:, 0, 0:386], ACT.Copy).then_inc(s_const, 1)
            for step in PLAN:
                kind = step[0]
                if kind == "square":
                    t = step[1]
                    act.wait_ge(s_x[t % 4], 16 * (t // 4 + 1))
                    if t:
                        act.wait_ge(s_xsq, t)
                    if t >= 2:
                        act.wait_ge(s_xn, t - 1)
                    nc.scalar.activation(rbuf[:, 0, 0:SEQ], xt[t % 4], ACT.Square,
                                         accum_out=xs[:, t % 2, 0:1]).then_inc(s_xsq, 1)
                if kind == "x":
                    t = step[1]
                    for u in range(2):
                        m = TURN0[step] + u
                        act.wait_ge(s_turn, m + 1)
                        nc.scalar.activation(hT[0][:, 4 * u:4 * u + 4, t * P:(t + 1) * P],
                                             psT[:, m % 2, :].rearrange("p (k q) -> p k q", k=4),
                                             ACT.Copy).then_inc(s_hi, 1)
                if kind == "forget":
                    act.wait_ge(s_wf, 16)
                    nc.scalar.activation(wf_hl[0], wf_raw, ACT.Copy).then_inc(s_fa, 1)
                    act.wait_ge(s_fd, 3)
                    nc.scalar.activation(f_rows[2], f_rows[1], ACT.Abs).then_inc(s_fa, 1)
                    act.wait_ge(s_fa, 2)
                    nc.scalar.activation(f_rows[2], f_rows[2], ACT.Exp, scale=-1.0).then_inc(s_fa, 1)
                    act.wait_ge(s_fa, 3)
                    nc.scalar.activation(f_rows[3], f_rows[2], ACT.Ln, bias=1.0).then_inc(s_fa, 1)
                if kind in ("weights", "wout"):
                    for i in range(1 if kind == "weights" else 2):
                        c = wchunk(step) + i
                        if kind == "weights":
                            dst = by_head(wpair[0][:, step[2], :])
                            src = wraw[:, c % 3, :].rearrange("p (f h c) -> p f h c", f=4, h=2)
                            if step[1]:
                                act.wait_ge(s_wk, KT * (step[1] - 1) + step[2] + 1)
                        else:
                            dst = wo[0][:, step[2], i * HALF:(i + 1) * HALF]
                            src = wraw[:, c % 3, :]
                            if step[2] == 0:
                                act.wait_ge(s_wk, KT * PAIRS)
                        act.wait_ge(s_wld[c % 3], 16 * (c // 3 + 1))
                        nc.scalar.activation(dst, src, ACT.Copy).then_inc(s_whi, 1)
                if kind == "raw":
                    _, j, t = step
                    i = j * TT + t
                    if t < TT - 1:
                        act.wait_ge(s_proj, j * (TT - 1) + t + 1)
                    else:
                        act.wait_ge(s_wk, KT * (j + 1))
                    if t % 4 == 0 and j:
                        act.wait_ge(s_vlo, VGATE[j - 1, 1, t // 4] + 1)
                        act.wait_ge(s_gate, VGATE[j - 1, 1, t // 4] + 1)
                        norms = NORM[j - 1, t // 4] + 1
                        if j <= PPG:
                            act.wait_ge(s_qc, norms)
                        else:
                            act.wait_ge(s_qn, norms - NORM_A)
                    if j == 0:
                        act.wait_ge(s_turn, 2 * (t // 2 + 5))
                    nc.scalar.activation(raw[:, t, :], psP[:, :], ACT.Copy).then_inc(s_raw, 1)
                if kind == "stats":
                    _, j, u = step
                    act.wait_ge(s_turn, last_turn(("heads", j - 1, 1, u)))
                    act.wait_ge(s_raw, TT * j + 4 * u + 4)
                    nc.scalar.activation(qks[:, :, 4 * u:4 * u + 4, :, :].rearrange("p s t f c -> p t s (f c)"),
                                         raw[:, 4 * u:4 * u + 4, :].rearrange("p t (s c) -> p t s c", s=2)[:, :, :, 0:P],
                                         ACT.Square).then_inc(s_sq, 1)
                if kind == "heads":
                    _, j, s, u = step
                    g = j // PPG
                    m = TURN0[step]
                    cols = slice(u * HALF, (u + 1) * HALF)
                    last = (j - 1) * 2 * TT + (s + 1) * TT
                    if j:
                        act.wait_ge(s_scores, last)
                    else:
                        act.wait_ge(s_fd, 1)
                    act.wait_ge(s_turn, m + 1)
                    nc.scalar.activation(stack[0:HD, s, 0, cols], psT[0:HD, m % 2, :], ACT.Copy,
                                         scale=gain[0:HD, g:g + 1])
                    nc.scalar.activation(stack[0:HD, s, 1, cols], psT[HD:P, m % 2, :], ACT.Copy,
                                         scale=gain[HD:P, g:g + 1])
                    nc.scalar.activation(stack[HD:P, s, 2, cols], psT[HD:P, m % 2, :], ACT.Copy,
                                         scale=gain[HD:P, g:g + 1]).then_inc(s_hi, 1)
                if kind == "vgate":
                    _, j, s, u = step
                    last = (j - 1) * 2 * TT + (s + 1) * TT
                    if j:
                        act.wait_ge(s_pv, CHUNK0[last])
                    nc.scalar.activation(vst[:, s, 4 * u:4 * u + 4, 0:HD], part(2, s, u), ACT.Copy).then_inc(s_vhi, 1)
                    if j:
                        act.wait_ge(s_evac, last_turn(("fold", last - TT + 4 * u + 3)))
                    nc.scalar.activation(gate[:, s, 4 * u:4 * u + 4, :], part(3, s, u), ACT.Tanh,
                                         scale=0.5).then_inc(s_ge, 1)
                if kind == "scores":
                    n = step[1]
                    off, _ = score_parts(n)
                    w = window(n)[1] * P
                    src = psS[:, n % 2, off:off + w]
                    q = n % 4
                    if group(n) == 0:
                        if n >= 2:
                            act.wait_ge(s_turn, turned(n - 2))
                        else:
                            act.wait_ge(s_fd, 4)
                        act.wait_ge(s_scores, n + 1)
                        nc.scalar.activation(zbuf[:, n % 2, 0:w], src, ACT.Sigmoid)
                        nc.scalar.activation(rbuf[:, n % 2, 0:w], src, ACT.Sigmoid, scale=-1.0).then_inc(s_sig, 1)
                    else:
                        act.wait_ge(s_nm, nslot(n)[1] + 1)
                        if n >= 4 + 2 * TT * PPG:
                            act.wait_ge(s_rd, nslot(n)[1] - 3)
                        nc.scalar.activation(zbuf[:, n % 2, 0:w], zbuf[:, n % 2, 0:w], ACT.Exp,
                                             bias=small[:, q, 1:2], accum_out=small[:, q, 2:3]).then_inc(s_exp, 1)
                if kind == "values":
                    n = step[1]
                    act.wait_ge(s_pv, CHUNK0[n + 1])
                    nc.scalar.activation(ocopy[:, :], psO[:, 0:P], ACT.Copy).then_inc(s_oc, 1)
                if kind == "turn":
                    _, n, u = step
                    nb = chunks(n)[u][1]
                    m = TURN0[step]
                    ci = CHUNK0[n] + u
                    if ci >= RING:
                        act.wait_ge(s_pv, ci - RING + 1)
                    act.wait_ge(s_turn, m + 1)
                    nc.scalar.activation(pt[:, ci % RING, 0:nb, 0, :],
                                         psT[:, m % 2, 0:nb * P].rearrange("p (b q) -> p b q", b=nb),
                                         ACT.Copy).then_inc(s_hi, 1)
                if kind == "mixed":
                    t = step[1]
                    if t == 0:
                        act.wait_ge(s_scores, NB)
                    if t >= 2:
                        act.wait_ge(s_oacc, t - 1)
                    for u in range(MT // 4):
                        m = TURN0[step] + u
                        act.wait_ge(s_turn, m + 1)
                        nc.scalar.activation(mixT[t % 2][0][:, u * HALF:(u + 1) * HALF], psT[:, m % 2, :],
                                             ACT.Copy).then_inc(s_hi, 1)

        @block.vector
        def _(dve):
            nc.vector.memset(gain[0:HD, 0:1], HD ** -0.5)
            nc.vector.memset(gain[HD:P, 0:1], 1.0).then_inc(s_revd, 1)
            dve.wait_ge(s_gain, 6 * 16)
            dve.wait_ge(s_revd, 1)
            nc.vector.tensor_scalar(gain[0:HD, 1:3], gain[0:HD, 1:3], HD ** -0.5, None, ALU.mult).then_inc(s_fd, 1)
            dve.wait_ge(s_rev, 16)
            nc.vector.tensor_copy(rev_row[:, 0:HALF], rel_row[:, RELW - 2:RELW - 1].broadcast_to([HG, HALF]))
            nc.vector.tensor_copy(rev_row[:, HALF:HALF + RELW - 2], rel_row[:, 0:RELW - 2][:, ::-1])
            nc.vector.memset(rev_row[:, HALF + RELW - 2:REVW], 0.0).then_inc(s_revd, 1)
            for step in PLAN:
                kind = step[0]
                if kind == "square":
                    t = step[1]
                    dve.wait_ge(s_xsq, t + 1)
                    nc.vector.tensor_scalar(xs[:, t % 2, 0:1], xs[:, t % 2, 0:1], 1.0 / DM, EPS, ALU.mult,
                                            ALU.add).then_inc(s_ms, 1)
                    dve.wait_ge(s_rs, t + 1)
                    nc.vector.scalar_tensor_tensor(out=xt[t % 4], in0=xt[t % 4], scalar=xs[:, t % 2, 1:2], in1=gx,
                                                   op0=ALU.mult, op1=ALU.mult).then_inc(s_xn, 1)
                if kind == "x":
                    t = step[1]
                    for u in range(2):
                        m = TURN0[step] + u
                        dve.wait_ge(s_hi, HI0[step] + u + 1)
                        ks, q = slice(4 * u, 4 * u + 4), slice(t * P, (t + 1) * P)
                        nc.vector.tensor_tensor(hT[1][:, ks, q], psT[:, m % 2, :].rearrange("p (k q) -> p k q", k=4),
                                                hT[0][:, ks, q].bitcast(F32), ALU.subtract).then_inc(s_evac, 1)
                if kind == "forget":
                    dve.wait_ge(s_fa, 1)
                    nc.vector.tensor_tensor(wf_hl[1], wf_raw, wf_hl[0].bitcast(F32), ALU.subtract).then_inc(s_fd, 1)
                    dve.wait_ge(s_f, 1)
                    nc.vector.tensor_scalar(f_rows[1], psS[0:HG, 0, :], bf[:, 0:1], -1.0, ALU.add,
                                            ALU.mult).then_inc(s_fd, 1)
                    dve.wait_ge(s_fa, 4)
                    nc.vector.scalar_tensor_tensor(out=f_rows[2], in0=f_rows[1], scalar=0.0, in1=f_rows[3],
                                                   op0=ALU.max, op1=ALU.add).then_inc(s_sp, 1)
                    dve.wait_ge(s_sp, 1)
                    nc.vector.tensor_tensor_scan(out=f_rows[0], data0=f_rows[2], data1=f_rows[2], initial=0.0,
                                                 op0=ALU.add, op1=ALU.bypass).then_inc(s_fd, 1)
                if kind in ("weights", "wout"):
                    for i in range(1 if kind == "weights" else 2):
                        c = wchunk(step) + i
                        if kind == "weights":
                            hi, lo = (by_head(w[:, step[2], :]) for w in wpair)
                            src = wraw[:, c % 3, :].rearrange("p (f h c) -> p f h c", f=4, h=2)
                        else:
                            hi, lo = (w[:, step[2], i * HALF:(i + 1) * HALF] for w in wo)
                            src = wraw[:, c % 3, :]
                        dve.wait_ge(s_whi, c + 1)
                        nc.vector.tensor_tensor(lo, src, hi.bitcast(F32), ALU.subtract).then_inc(s_wlo, 1)
                if kind == "stats":
                    _, j, u = step
                    i = 2 * (j - PPG) + u
                    half = ms[:, 16 * u:16 * u + 16]
                    dve.wait_ge(s_sq, i + 1)
                    for s in range(2):
                        ins = nc.vector.tensor_reduce(half[:, 8 * s:8 * s + 8], qks[:, s, 4 * u:4 * u + 4, :, :].rearrange(
                            "p t f c -> p (t f) c"), AX.X, ALU.add)
                    ins.then_inc(s_sum, 1)
                    dve.wait_ge(s_sum, i + 1)
                    nc.vector.tensor_scalar(half, half, 1.0 / HD, EPS, ALU.mult, ALU.add).then_inc(s_ss, 1)
                if kind == "norm" and step[1] >= PPG:
                    _, j, u = step
                    dve.wait_ge(s_rs, TT + NORM[j, u] - NORM_A + 1)
                    for s in range(2):
                        r = rs[:, 16 * u + 8 * s:16 * u + 8 * s + 8].rearrange("p (t f) -> p t f", f=2)
                        for f in range(2):
                            ins = nc.vector.tensor_tensor(qks[:, s, 4 * u:4 * u + 4, f, :], part(f, s, u),
                                                          r[:, :, f:f + 1].broadcast_to([P, TT // 2, HD]), ALU.mult)
                    ins.then_inc(s_qn, 1)
                if kind == "heads":
                    _, j, s, u = step
                    g = j // PPG
                    m = TURN0[step]
                    cols = slice(u * HALF, (u + 1) * HALF)
                    dve.wait_ge(s_hi, HI0[step] + 1)
                    nc.vector.scalar_tensor_tensor(
                        out=stack[HD:P, s, 0, cols], in0=psT[0:HD, m % 2, :], scalar=gain[0:HD, g:g + 1],
                        in1=stack[0:HD, s, 0, cols].bitcast(F32), op0=ALU.mult, op1=ALU.subtract)
                    nc.vector.scalar_tensor_tensor(
                        out=stack[HD:P, s, 1, cols], in0=psT[HD:P, m % 2, :], scalar=gain[HD:P, g:g + 1],
                        in1=stack[HD:P, s, 2, cols].bitcast(F32), op0=ALU.mult, op1=ALU.subtract)
                    nc.vector.scalar_tensor_tensor(
                        out=stack[0:HD, s, 2, cols], in0=psT[HD:P, m % 2, :], scalar=gain[HD:P, g:g + 1],
                        in1=stack[HD:P, s, 2, cols].bitcast(F32), op0=ALU.mult, op1=ALU.subtract
                    ).then_inc(s_evac, 1)
                if kind == "vgate":
                    _, j, s, u = step
                    i = VGATE[j, s, u]
                    dve.wait_ge(s_vhi, i + 1)
                    nc.vector.tensor_tensor(vst[:, s, 4 * u:4 * u + 4, HD:P], part(2, s, u),
                                            vst[:, s, 4 * u:4 * u + 4, 0:HD].bitcast(F32), ALU.subtract).then_inc(s_vlo, 1)
                    gh = gate[:, s, 4 * u:4 * u + 4, :]
                    dve.wait_ge(s_ge, i + 1)
                    nc.vector.scalar_tensor_tensor(out=gh, in0=gh, scalar=1.0, in1=part(3, s, u), op0=ALU.add,
                                                   op1=ALU.mult).then_inc(s_gate, 1)
                if kind == "scores":
                    n = step[1]
                    off, _ = score_parts(n)
                    w = window(n)[1] * P
                    q = n % 4
                    if group(n) == 0:
                        dve.wait_ge(s_sig, n + 1)
                        rem = rbuf[:, n % 2, 0:w]
                        nc.vector.memset(rbuf[:, n % 2, w:w + 1], 1.0).then_inc(s_rem, 1)
                        back = rem[:, ::-1]
                        nc.vector.tensor_tensor_scan(out=back, data0=back, data1=back, initial=1.0,
                                                     op0=ALU.mult, op1=ALU.bypass).then_inc(s_rem, 1)
                        dve.wait_ge(s_rem, 2 * n + 2)
                        nc.vector.tensor_tensor(zbuf[:, n % 2, 0:w], zbuf[:, n % 2, 0:w],
                                                rbuf[:, n % 2, 1:w + 1], ALU.mult).then_inc(s_w, 1)
                    else:
                        i = nslot(n)[1]
                        if n % TT == 0:
                            dve.wait_ge(s_bias[slot(n)], 16 * bias_loads(n))
                            if group(n) == 1:
                                dve.wait_ge(s_corner, 2 * (n // TT - 2 * PPG + 1))
                        dve.wait_ge(s_turn, turned(n - 2))
                        dve.wait_ge(s_scores, n + 1)
                        if i >= 4:
                            dve.wait_ge(s_exp, i - 3)
                        add = bias[:, slot(n), 0:w] if group(n) == 2 else bias[:, slot(n), P * WIN - w:P * WIN]
                        nc.vector.tensor_tensor_reduce(out=zbuf[:, n % 2, 0:w], in0=psS[:, n % 2, off:off + w],
                                                       in1=add, scale=1.0, scalar=-3.0e38, op0=ALU.add, op1=ALU.max,
                                                       accum_out=small[:, q, 0:1]).then_inc(s_z, 1)
                        dve.wait_ge(s_z, i + 1)
                        nc.vector.tensor_scalar(small[:, q, 1:2], small[:, q, 0:1], -1.0, None,
                                                ALU.mult).then_inc(s_nm, 1)
                if kind == "values":
                    n = step[1]
                    if n >= 2:
                        dve.wait_ge(s_turn, last_turn(("fold", n - 2)))
                    dve.wait_ge(s_oc, n + 1)
                    nc.vector.tensor_tensor(osum[:, n % 2, :], psO[:, P:2 * P], ocopy[:, :], ALU.add).then_inc(s_os, 1)
                if kind == "turn":
                    _, n, u = step
                    nb = chunks(n)[u][1]
                    m = TURN0[step]
                    ci = CHUNK0[n] + u
                    dve.wait_ge(s_hi, HI0[step] + 1)
                    nc.vector.tensor_tensor(pt[:, ci % RING, 0:nb, 1, :],
                                            psT[:, m % 2, 0:nb * P].rearrange("p (b q) -> p b q", b=nb),
                                            pt[:, ci % RING, 0:nb, 0, :].bitcast(F32),
                                            ALU.subtract).then_inc(s_evac, 1)
                if kind == "fold":
                    n = step[1]
                    b = n % TT
                    s = slot(n)
                    m = TURN0[step]
                    if b % 4 == 0:
                        if n >= 2 * TT:
                            dve.wait_ge(s_mo[2 * (b // 4) + s], 16 * (n // (2 * TT)))
                        dve.wait_ge(s_gate, VGATE[n // (2 * TT), s, b // 4] + 1)
                    if group(n):
                        i = nslot(n)[1]
                        dve.wait_ge(s_exp, i + 1)
                        nc.vector.reciprocal(small[:, n % 4, 3:4], small[:, n % 4, 2:3]).then_inc(s_rd, 1)
                        dve.wait_ge(s_rd, i + 1)
                    dve.wait_ge(s_turn, m + 1)
                    src = psT[:, m % 2, 0:HD]
                    if group(n):
                        nc.vector.scalar_tensor_tensor(out=mo[:, s, b, :], in0=src, scalar=small[:, n % 4, 3:4],
                                                       in1=gate[:, s, b, :], op0=ALU.mult,
                                                       op1=ALU.mult).then_inc(s_evac, 1)
                    else:
                        nc.vector.tensor_tensor(mo[:, s, b, :], src, gate[:, s, b, :], ALU.mult).then_inc(s_evac, 1)
                if kind == "mixed":
                    t = step[1]
                    for u in range(MT // 4):
                        m = TURN0[step] + u
                        dve.wait_ge(s_hi, HI0[step] + u + 1)
                        nc.vector.tensor_tensor(mixT[t % 2][1][:, u * HALF:(u + 1) * HALF], psT[:, m % 2, :],
                                                mixT[t % 2][0][:, u * HALF:(u + 1) * HALF].bitcast(F32),
                                                ALU.subtract).then_inc(s_evac, 1)
                if kind == "out":
                    t = step[1]
                    dve.wait_ge(s_oacc, t + 1)
                    dve.wait_ge(s_xr[t % 2], 16 * (t // 2 + 1))
                    if t < 2:
                        dve.wait_ge(s_w, 2 * TT * PPG)
                    else:
                        dve.wait_ge(s_out[t % 2], 16 * (t // 2))
                    nc.vector.tensor_tensor(rbuf[:, t % 2, 0:SEQ], psS[:, t % 2, :], zbuf[:, t % 2, :],
                                            ALU.add).then_inc(s_res, 1)

        @block.tensor
        def _(pe):
            pe.wait_ge(s_const, 11)
            for step in PLAN:
                kind = step[0]
                if kind == "x":
                    t = step[1]
                    pe.wait_ge(s_xn, t + 1)
                    for u in range(2):
                        m = TURN0[step] + u
                        if m >= 2:
                            pe.wait_ge(s_evac, m - 1)
                        for i in range(4):
                            ins = nc.tensor.transpose(psT[:, m % 2, i * P:(i + 1) * P],
                                                      xt[t % 4][:, (4 * u + i) * P:(4 * u + i + 1) * P], ident[:, :])
                        ins.then_inc(s_turn, 1)
                if kind == "forget":
                    pe.wait_ge(s_fd, 2)
                    pe.wait_ge(s_evac, 2 * TT)
                    for u in range(2):
                        for i, (a, b) in enumerate(((0, 0), (0, 1), (1, 0))):
                            for k in range(KT):
                                ins = nc.tensor.matmul(psS[0:HG, 0, u * HALF:(u + 1) * HALF], wf_hl[a][:, k, :],
                                                       hT[b][:, k, u * HALF:(u + 1) * HALF],
                                                       start=(i == 0 and k == 0), stop=(i == 2 and k == KT - 1))
                    ins.then_inc(s_f, 1)
                if kind == "project":
                    _, j, t, k0, k1 = step
                    i = j * TT + t
                    if i and k0 == 0:
                        pe.wait_ge(s_raw, i)
                    if j == 0 and k0 == 0:
                        pe.wait_ge(s_evac, last_turn(("x", t)))
                    for k in range(k0, k1):
                        if t == 0:
                            pe.wait_ge(s_wlo, KT * j + k + 1)
                        for q, (a, b) in enumerate(((0, 0), (0, 1), (1, 0))):
                            ins = nc.tensor.matmul(psP[:, :], hT[a][:, k, t * P:(t + 1) * P], wpair[b][:, k, :],
                                                   start=(k == 0 and q == 0), stop=(k == KT - 1 and q == 2))
                        if t == TT - 1:
                            ins.then_inc(s_wk, 1)
                    if k1 == KT and t < TT - 1:
                        ins.then_inc(s_proj, 1)
                if kind == "heads":
                    _, j, s, u = step
                    m = TURN0[step]
                    if j < PPG:
                        pe.wait_ge(s_qc, NORM[j, u] + 1)
                    else:
                        pe.wait_ge(s_qn, NORM[j, u] - NORM_A + 1)
                    pe.wait_ge(s_evac, m - 1)
                    for i in range(4):
                        t = 4 * u + i
                        ins = nc.tensor.transpose(psT[:, m % 2, i * P:(i + 1) * P],
                                                  qks[:, s, t, :, :].rearrange("p f c -> p (f c)"), ident[:, :])
                    ins.then_inc(s_turn, 1)
                if kind == "scores":
                    n = step[1]
                    s, b = slot(n), n % TT
                    if b % 4 == 0:
                        pe.wait_ge(s_evac, last_turn(("heads", n // (2 * TT), s, b // 4)))
                    if n >= 2:
                        a, bc = nslot(n - 1)
                        if group(n - 2):
                            pe.wait_ge(s_z, bc)
                        else:
                            pe.wait_ge(s_sig, a)
                    elif n == 0:
                        pe.wait_ge(s_fd, 3)
                    qs = stack[:, s, 0, b * P:(b + 1) * P]
                    off, parts = score_parts(n)
                    for pi, (col, key, w) in enumerate(parts):
                        dst = psS[:, n % 2, col:col + w]
                        last = pi == len(parts) - 1
                        masked = group(n) != 1 and last
                        nc.tensor.matmul(dst, qs, stack[:, s, 1, key:key + w], start=True, stop=False)
                        ins = nc.tensor.matmul(dst, qs, stack[:, s, 2, key:key + w], start=False, stop=not masked)
                        if masked:
                            end = off + P * (b + 1) if b else 256
                            m0 = (1 if b else 1 + P) - (group(n) == 2)
                            ins = nc.tensor.matmul(psS[:, n % 2, end - 256:end], identr[:, :], mask[:, m0:m0 + 256],
                                                   start=False, stop=True)
                    ins.then_inc(s_scores, 1)
                if kind == "values":
                    n = step[1]
                    s = slot(n)
                    k0, total = window(n)
                    if n % 4 == 0:
                        pe.wait_ge(s_vlo, VGATE[n // (2 * TT), s, n % TT // 4] + 1)
                    if n:
                        pe.wait_ge(s_os, n)
                    for u, (c, nb) in enumerate(chunks(n)):
                        ci = CHUNK0[n] + u
                        pe.wait_ge(s_evac, last_turn(("turn", n, u)))
                        for i in range(nb):
                            ins = nc.tensor.matmul(psO[:, 0:2 * P], vst[:, s, k0 + c + i, :],
                                                   pt[:, ci % RING, i, :, :], start=(c + i == 0),
                                                   stop=(c + i == total - 1))
                        ins.then_inc(s_pv, 1)
                if kind == "turn":
                    _, n, u = step
                    c, nb = chunks(n)[u]
                    m = TURN0[step]
                    a, bc = nslot(n + 1)
                    if group(n):
                        pe.wait_ge(s_exp, bc)
                    else:
                        pe.wait_ge(s_w, a)
                    pe.wait_ge(s_evac, m - 1)
                    for i in range(nb):
                        ins = nc.tensor.transpose(psT[:, m % 2, i * P:(i + 1) * P],
                                                  zbuf[:, n % 2, (c + i) * P:(c + i + 1) * P], ident[:, :])
                    ins.then_inc(s_turn, 1)
                if kind == "fold":
                    n = step[1]
                    m = TURN0[step]
                    pe.wait_ge(s_os, n + 1)
                    pe.wait_ge(s_evac, m - 1)
                    nc.tensor.matmul(psT[:, m % 2, 0:HD], osum[:, n % 2, :], foldm[:, :], start=True,
                                     stop=True).then_inc(s_turn, 1)
                if kind == "mixed":
                    t = step[1]
                    pe.wait_ge(s_mx[t % 2], 16 * (t // 2 + 1))
                    for u in range(MT // 4):
                        m = TURN0[step] + u
                        pe.wait_ge(s_evac, m - 1)
                        for i in range(4):
                            c = (t % 2) * DMIX + (4 * u + i) * P
                            ins = nc.tensor.transpose(psT[:, m % 2, i * P:(i + 1) * P], mixin[:, c:c + P], ident[:, :])
                        ins.then_inc(s_turn, 1)
                if kind == "out":
                    t = step[1]
                    pe.wait_ge(s_evac, last_turn(("mixed", t)))
                    if t == 0:
                        pe.wait_ge(s_wlo, PAIRS * KT + 2 * MT)
                        pe.wait_ge(s_z, NB - 2 * TT * PPG)
                    if t >= 2:
                        pe.wait_ge(s_res, t - 1)
                    for c in range(2):
                        for k in range(MT):
                            for q, (a, b) in enumerate(((0, 0), (0, 1), (1, 0))):
                                ins = nc.tensor.matmul(psS[:, t % 2, c * HALF:(c + 1) * HALF],
                                                       mixT[t % 2][a][:, k * P:(k + 1) * P],
                                                       wo[b][:, k, c * HALF:(c + 1) * HALF],
                                                       start=(k == 0 and q == 0), stop=(k == MT - 1 and q == 2))
                    ins.then_inc(s_oacc, 1)


_INS = ["x", "norm_g", "w_in", "b_forget", "q_norm_ch", "k_norm_ch", "q_norm_fox", "k_norm_fox", "rel_bias", "w_out"]


def kernel(**inputs):
    import numpy as _np
    import concourse.bacc as _bacc
    from concourse import mybir as _mybir
    from concourse.bass_utils import run_bass_kernel_spmd as _run

    nc = _bacc.Bacc("TRN2", target_bir_lowering=False, num_devices=1)
    arrays, args = {}, []
    for name in _INS:
        a = _np.ascontiguousarray(inputs[name])
        arrays[f"in_{name}_dram"] = a
        args.append(nc.dram_tensor(f"in_{name}_dram", a.shape, _mybir.dt.from_np(a.dtype), kind="ExternalInput").ap())
    args.append(nc.dram_tensor("out_0_dram", (1, SEQ, DM), _mybir.dt.float32, kind="ExternalOutput").ap())
    build(nc, *args)
    r = _run(nc, [arrays], core_ids=[0])
    return r.results[0]["out_0_dram"]
```

```python
from contextlib import ExitStack

import numpy as np
import concourse.bass as bass
from concourse import mybir

F32 = mybir.dt.float32
F32R = mybir.dt.float32r
ALU = mybir.AluOpType
ACT = mybir.ActivationFunctionType
AX = mybir.AxisListType

P = 128
SEQ = 1024
DM = 1024
HD = 64
HG = 8
WG = HG * HD
NGROUP = 3
DMIX = NGROUP * WG
RELW = 257
CHUNK = 64
WIN = 5
EPS = 1e-6
BIG_NEG = -1e30

KT = DM // P
TT = SEQ // P
MT = DMIX // P
MF = 8
PAIRS = NGROUP * HG // 2
PPG = HG // 2
NB = PAIRS * 2 * TT
HALF = 512
RING = 3
REVW = P * WIN + P


def group(n):
    return n // (2 * TT * PPG)


def slot(n):
    return (n // TT) % 2


def window(n):
    b = n % TT
    return (max(0, b - WIN + 1), min(b + 1, WIN)) if group(n) == 1 else (0, b + 1)


def score_parts(n):
    k0, nb = window(n)
    w = nb * P
    if w <= HALF:
        return 0, [(0, k0 * P, max(w, 256))]
    off = 256 if w == 640 else 0
    return off, [(off, k0 * P, HALF - off), (HALF, k0 * P + HALF - off, w + off - HALF)]


def chunks(n):
    nb = window(n)[1]
    return [(c, min(4, nb - c)) for c in range(0, nb, 4)]


CHUNK0 = [0]
for _n in range(NB):
    CHUNK0.append(CHUNK0[-1] + len(chunks(_n)))


HEADS_AT = {(0, 1): 1, (1, 0): 4, (1, 1): 3}
VGATE_AT = {(1, 0): 1, (0, 1): 3, (1, 1): 5}
NORM_AT = 0
AHEAD = {"stats": 9, "norm": 10, "heads": 11, "vgate": 9}


def extras(j, r):
    found = []
    if r == NORM_AT and j:
        found.append([("norm", j, 1)])
    if r == 0 and j + 1 < PAIRS:
        found.append([("weights", j + 1, KT - 2), ("weights", j + 1, KT - 1)])
    found += [[("vgate", j, s, u)] for (s, u), at in VGATE_AT.items() if at == r]
    found += [[("heads", j, s, u)] for (s, u), at in HEADS_AT.items() if at == r]
    if j + 1 < PAIRS:
        if r in (AHEAD["stats"], 15) and j + 1 >= PPG:
            found.append([("stats", j + 1, r // 15)])
        for kind in ("norm", "heads", "vgate"):
            if r == AHEAD[kind]:
                found.append([(kind, j + 1, 0) if kind == "norm" else (kind, j + 1, 0, 0)])
    if 13 <= r and j + 2 < PAIRS:
        found.append([("weights", j + 2, k) for k in (2 * (r - 13), 2 * (r - 13) + 1)])
    if j + 2 >= PAIRS:
        found += [[("wout", c)] for c, at in enumerate(WOUT_AT) if at == 2 * TT * (j + 1 - PAIRS) + r]
    if j + 1 == PAIRS and r == MIX_AT:
        found += [[("mixed", 0, 0, 0)], [("mixed", 0, 0, 1)]]
    return found


def plan():
    steps = [("square", 0), ("scale", 0), ("square", 1)]
    for t in range(TT):
        steps.append(("x", t))
        if t == 2:
            steps.append(("constants",))
        if t < 4:
            steps += [("weights", 0, 2 * t), ("weights", 0, 2 * t + 1)]
        if t + 1 < TT:
            steps.append(("scale", t + 1))
        if t + 2 < TT:
            steps.append(("square", t + 2))
        if 1 <= t <= 4:
            steps.append(("project", 0, 0, 2 * t - 2, 2 * t))
            if t == 4:
                steps.append(("raw", 0, 0))
        elif t > 4:
            steps += [("project", 0, t - 4, 0, KT), ("raw", 0, t - 4)]
    for t in range(4, TT):
        if t == 4:
            steps.append(("norm", 0, 0))
        steps += [("project", 0, t, 0, KT), ("raw", 0, t)]
        if t == 5:
            steps.append(("forget", 0))
        if t == 6:
            steps += [("heads", 0, 0, 0), ("vgate", 0, 0, 0)]
    steps.append(("norm", 0, 1))
    steps += [("weights", 1, k) for k in range(KT - 2)]
    for n in range(NB + 3):
        j, r = divmod(n, 2 * TT)
        kinds = {"S": [], "F": [], "V": [], "T": [], "X": [], "W": []}
        if n < NB:
            kinds["S"] = [[("scores", n)]]
            kinds["W"] = [[("weigh", n)]]
            kinds["X"] = extras(j, r)
        if n >= 3:
            kinds["F"] = [[("fold", n - 3)]]
        if 2 <= n < NB + 2:
            kinds["V"] = [[("values", n - 2)]]
        if 1 <= n < NB + 1:
            kinds["T"] = [[("turn", n - 1, u)] for u in range(len(chunks(n - 1)))]
        items = []
        for kind in ORDER:
            if kind == "W" and kinds[kind]:
                items[-1] = items[-1] + kinds[kind][0]
            else:
                items += kinds[kind]
        if r == 0 and n < NB:
            done = rest = 0
        for i, item in enumerate(items):
            steps += item
            if n < NB and j + 1 < PAIRS:
                t, k = divmod(done, KT)
                k1 = min(KT, k + UNIT0[r] + (i + 1) * UNITS[r] // len(items) - done)
                rest -= 1
                if k1 > k and rest < 0:
                    steps += [("project", j + 1, t, k, k1)] + ([("raw", j + 1, t)] if k1 == KT else [])
                    done += k1 - k
                    if k1 == KT:
                        rest = REST
            if n < NB and j + 1 == PAIRS:
                rest -= 1
                until = OUT_UNIT0[r] + (i + 1) * OUT_UNITS[r] // len(items)
                while done < until and rest < 0:
                    i2, k = divmod(done, MF)
                    k1 = min(MF, k + until - done)
                    steps.append(("first", i2, k, k1))
                    for mark, u in ((4, 0), (10, 1)):
                        at = 2 * MF * (i2 // 2) + mark
                        if done < at <= done + k1 - k and i2 // 2 + 1 < TT:
                            steps.append(("mixed", 0, i2 // 2 + 1, u))
                    done += k1 - k
                    if k1 == MF:
                        steps.append(("part", i2))
                        rest = REST
    steps += [("mixed", 1, 0, 0)] + [("wout", c) for c in range(2 * MT - 4, 2 * MT)]
    for t in range(TT):
        if t + 1 < TT:
            steps.append(("mixed", 1, t + 1, 0))
        steps.append(("out", t))
    return steps


UNITS = [2, 8, 7, 1, 6, 6, 4, 3, 3, 3, 7, 2, 4, 3, 5, 0]
REST = 2
OUT_UNITS = [0, 1, 5, 6, 11, 10, 8, 7, 9, 10, 11, 10, 11, 9, 10, 10]
WOUT_AT = [-1, -1, -1, 0, 0, 0, 0, 1, 1, 1, 1, 2, 2, 2, 2, 3, 3, 3, 4, 4]
MIX_AT = 0
OUT_UNIT0 = [sum(OUT_UNITS[:r]) for r in range(2 * TT + 1)]
assert OUT_UNIT0[-1] == 2 * TT * MF
WR = 4
XB = 6
ORDER = "SFWVTX"
UNIT0 = [sum(UNITS[:r]) for r in range(2 * TT + 1)]
assert UNIT0[-1] == KT * TT

PLAN = plan()


def turns_of(step):
    if step[0] == "x":
        return 2
    if step[0] == "heads":
        return 1
    if step[0] == "turn":
        return 1
    if step[0] == "fold":
        return 1
    if step[0] == "mixed":
        return 1
    return 0


TURN0, HI0 = {}, {}
_t = _h = 0
for _s in PLAN:
    TURN0[_s], HI0[_s] = _t, _h
    _t += turns_of(_s)
    _h += turns_of(_s) if _s[0] != "fold" else 0


VGATE = {s[1:]: i for i, s in enumerate(s for s in PLAN if s[0] == "vgate")}
NORM = {s[1:]: i for i, s in enumerate(s for s in PLAN if s[0] == "norm")}
NORM_A = 2 * PPG


def wchunk(step):
    if step[0] == "weights":
        return step[1] * KT + step[2]
    return PAIRS * KT + step[1]


def build(nc, x, norm_g, w_in, b_forget, q_norm_ch, k_norm_ch, q_norm_fox, k_norm_fox, rel_bias, w_out, out):
    decay_d = nc.dram_tensor("decay_scratch", (HG, SEQ), F32).ap()
    rev_d = nc.dram_tensor("bias_scratch", (HG, REVW), F32).ap()
    skew_d = nc.dram_tensor("skew_scratch", (HG, P, REVW), F32).ap()
    mix_d = nc.dram_tensor("mixed_scratch", (SEQ, DMIX), F32).ap()
    part_d = nc.dram_tensor("part_scratch", (SEQ, DM), F32).ap()

    with ExitStack() as ctx:
        def sb(name, shape, dt=F32):
            return ctx.enter_context(nc.sbuf_tensor(name, shape, dt))

        def sem(name):
            return ctx.enter_context(nc.semaphore(name))

        big = sb("big", [P, 2 * MT * DM], F32R)
        hT = [big[:, i * KT * SEQ:(i + 1) * KT * SEQ].rearrange("p (k s) -> p k s", k=KT) for i in range(2)]
        w0 = 2 * KT * SEQ
        wpair = [big[:, w0 + i * KT * HALF:w0 + (i + 1) * KT * HALF].rearrange("p (k c) -> p k c", k=KT)
                 for i in range(2)]
        wo = [big[:, i * MT * DM:(i + 1) * MT * DM].rearrange("p (k c) -> p k c", k=MT) for i in range(2)]
        wraw = sb("wraw", [P, WR, HALF])
        raw = sb("raw", [P, TT, HALF])
        stack = sb("stack", [P, 2, 3, SEQ], F32R)
        vst = sb("vst", [P, 2, TT, P], F32R)
        qks = sb("qks", [P, 2, TT, 2, HD])
        gate = sb("gate", [P, 2, TT, HD])
        zbuf = sb("zbuf", [P, 2, SEQ])
        rbuf = sb("rbuf", [P, 2, SEQ + 1])
        bias = sb("bias", [P, 2, SEQ])
        pt = sb("pt", [P, RING, 4, 2, P], F32R)
        mo = sb("mo", [P, 2, TT, HD])
        identr = sb("identr", [P, P], F32R)
        ident = identr[:, :].bitcast(F32)
        foldm = sb("foldm", [P, HD])
        mask = sb("mask", [P, 386], F32R)
        osum = sb("osum", [P, 2, P])
        gain = sb("gain", [P, NGROUP])
        small = sb("small", [P, 4, 4])
        xs = sb("xs", [P, 4, 2])
        ms = sb("ms", [P, 32])
        rs = sb("rs", [P, 32])
        mhalf = sb("mhalf", [P, 32])
        bf = sb("bf", [HG, 1])

        psS = ctx.enter_context(nc.psum_tensor("psS", [P, 2, 2 * HALF], F32))
        psT = ctx.enter_context(nc.psum_tensor("psT", [P, 2, HALF], F32))
        psO = ctx.enter_context(nc.psum_tensor("psO", [P, HALF], F32))
        psP = ctx.enter_context(nc.psum_tensor("psP", [P, HALF], F32))

        mixF = [rbuf[:, i, 0:MF * P] for i in range(2)]
        mixFT = [[big[:, (i * MT + MT - 2) * DM + q * MF * P:(i * MT + MT - 2) * DM + (q + 1) * MF * P]
                  for i in range(2)] for q in range(2)]
        piece = [raw[:, i, :] for i in range(4)]
        mixL = [qks[:, :, :, :, :].rearrange("p s t f c -> p (s t f c)"), zbuf[:, :, :].rearrange("p a b -> p (a b)")]
        mixLT = [[stack[:, 0, i, q * HALF:(q + 1) * HALF] for i in range(2)] for q in range(2)]
        total = [raw[:, 4:6, :].rearrange("p a b -> p (a b)"), raw[:, 6:8, :].rearrange("p a b -> p (a b)"),
                 rbuf[:, 0, 0:SEQ], rbuf[:, 1, 0:SEQ]]

        s_const = sem("s_const")
        s_gx = sem("s_gx")
        s_gain = sem("s_gain")
        s_x = [sem(f"s_x{i}") for i in range(XB)]
        s_xsq = sem("s_xsq")
        s_ms = sem("s_ms")
        s_rs = sem("s_rs")
        s_xn = sem("s_xn")
        s_wld = [sem(f"s_wld{i}") for i in range(WR)]
        s_whi = sem("s_whi")
        s_wlo = sem("s_wlo")
        s_turn = sem("s_turn")
        s_hi = sem("s_hi")
        s_evac = sem("s_evac")
        s_proj = sem("s_proj")
        s_wk = sem("s_wk")
        s_raw = sem("s_raw")
        s_sq = sem("s_sq")
        s_sum = sem("s_sum")
        s_ss = sem("s_ss")
        s_qc = sem("s_qc")
        s_qn = sem("s_qn")
        s_vhi = sem("s_vhi")
        s_vlo = sem("s_vlo")
        s_ge = sem("s_ge")
        s_gate = sem("s_gate")
        s_scores = sem("s_scores")
        s_sig = sem("s_sig")
        s_rem = sem("s_rem")
        s_w = sem("s_w")
        s_z = sem("s_z")
        s_nm = sem("s_nm")
        s_exp = sem("s_exp")
        s_pv = sem("s_pv")
        s_oc = sem("s_oc")
        s_os = sem("s_os")
        s_rd = sem("s_rd")
        s_mo = [sem(f"s_mo{i}") for i in range(4)]
        s_bias = [sem("s_bias0"), sem("s_bias1")]
        s_corner = sem("s_corner")
        s_f = sem("s_f")
        s_fd = sem("s_fd")
        s_fa = sem("s_fa")
        s_sp = sem("s_sp")
        s_wf = sem("s_wf")
        s_scr = sem("s_scr")
        s_skew = sem("s_skew")
        s_rev = sem("s_rev")
        s_revd = sem("s_revd")
        s_mxf = [sem("s_mxf0"), sem("s_mxf1")]
        s_xr = [sem(f"s_xr{i}") for i in range(4)]
        s_first = sem("s_first")
        s_half = sem("s_half")
        s_part = [sem(f"s_part{i}") for i in range(4)]
        s_mxl = [sem("s_mxl0"), sem("s_mxl1")]
        s_tot = [sem(f"s_tot{i}") for i in range(4)]
        s_oacc = sem("s_oacc")
        s_res = sem("s_res")
        s_out = [sem(f"s_out{i}") for i in range(4)]

        wf_hl = [pt[:, 0, i, 0, 0:KT * HG].rearrange("p (k c) -> p k c", k=KT) for i in range(2)]
        f_rows = [bias[0:HG, 0, :], bias[0:HG, 1, :], rbuf[0:HG, 0, 0:SEQ], rbuf[0:HG, 1, 0:SEQ]]
        rel_row = osum[0:HG, :, :].rearrange("p a b -> p (a b)")
        mo_flat = mo[:, :, :, :].rearrange("p a b c -> p (a b c)")
        rev_row = mo_flat[0:HG, 0:REVW]
        ident_raw = mo_flat[:, REVW:REVW + P]
        wf_raw = mo_flat[:, REVW + P:REVW + P + KT * HG].rearrange("p (k c) -> p k c", k=KT)
        gx = bias[:, 1, :]
        xt = [zbuf[:, 0, :], zbuf[:, 1, :], qks[:, 0, :, :, :].rearrange("p t f c -> p (t f c)"),
              qks[:, 1, :, :, :].rearrange("p t f c -> p (t f c)"), gate[:, :, :, :].rearrange("p s t c -> p (s t c)"),
              rbuf[:, 1, 0:SEQ]]

        def by_head(w):
            return w.rearrange("p (h f c) -> p f h c", h=2, f=4)

        def part(f, s, u):
            return raw[:, 4 * u:4 * u + 4, (4 * s + f) * HD:(4 * s + f + 1) * HD]

        def nslot(n):
            a = 2 * TT * PPG
            return min(n, a), max(0, n - a)

        def last_turn(step):
            return TURN0[step] + turns_of(step)

        def turned(n):
            return last_turn(("turn", n, len(chunks(n)) - 1))

        def bias_loads(n):
            return n // (2 * TT) - PPG + 1

        block = ctx.enter_context(nc.Block())

        @block.sync
        def _(sp):
            def load_first(t):
                if t % 4 == 0:
                    sp.wait_ge(s_mo[t // 2], 16 * MF)
                    sp.wait_ge(s_mo[t // 2 + 1], 16 * MF)
                if t >= 2:
                    sp.wait_ge(s_turn, last_turn(("mixed", 0, t - 2, 1)))
                sp.dma_start(mixF[t % 2], mix_d[t * P:(t + 1) * P, 0:MF * P]).then_inc(s_mxf[t % 2], 16)

            def load_residual(i):
                t, c = divmod(i, 2)
                if i >= 4:
                    sp.wait_ge(s_part[i % 4], 16 * (i // 4))
                sp.dma_start(piece[i % 4], x[0, t * P:(t + 1) * P, c * HALF:(c + 1) * HALF]).then_inc(s_xr[i % 4], 16)

            def load_last(u):
                sp.wait_ge(s_mo[2 * u], 16 * PAIRS)
                sp.wait_ge(s_mo[2 * u + 1], 16 * PAIRS)
                src = mix_d[u * HALF:(u + 1) * HALF, MF * P:DMIX].rearrange("(t p) c -> p t c", p=P)
                sp.dma_start(mixL[u].rearrange("p (t c) -> p t c", t=4), src).then_inc(s_mxl[u], 16)

            def load_total(t):
                sp.dma_start(total[t % 4], part_d[t * P:(t + 1) * P, :]).then_inc(s_tot[t % 4], 16)

            def load_weights(c):
                if c < PAIRS * KT:
                    j, k = divmod(c, KT)
                    g, jj = divmod(j, PPG)
                    src = w_in[0, k * P:(k + 1) * P, g * 4 * WG:(g + 1) * 4 * WG].rearrange(
                        "p (f c) -> p f c", f=4)[:, :, jj * P:(jj + 1) * P]
                    dst = wraw[:, c % WR, :].rearrange("p (f c) -> p f c", f=4)
                elif c < PAIRS * KT + 2 * MT:
                    k, i = divmod(c - PAIRS * KT, 2)
                    src = w_out[0, k * P:(k + 1) * P, i * HALF:(i + 1) * HALF]
                    dst = wraw[:, c % WR, :]
                else:
                    return
                if c >= WR:
                    sp.wait_ge(s_wlo, c - WR + 1)
                sp.dma_start(dst, src).then_inc(s_wld[c % WR], 16)

            def load_x(t):
                sp.dma_start(xt[t % XB], x[0, t * P:(t + 1) * P, :]).then_inc(s_x[t % XB], 16)

            load_x(0)
            sp.dma_start(gx, norm_g[0:1, :].broadcast_to([P, DM])).then_inc(s_gx, 16)
            load_weights(0)
            load_weights(1)
            load_x(1)
            for c in range(2, WR):
                load_weights(c)
            load_x(2)
            with nc.allow_non_contiguous_dma(reason="the gains, once"):
                for t, (q, k) in enumerate(((q_norm_ch, k_norm_ch), (q_norm_fox, k_norm_fox))):
                    sp.dma_start(gain[0:HD, t + 1:t + 2], q.rearrange("a d -> d a")).then_inc(s_gain, 16)
                    sp.dma_start(gain[HD:P, t + 1:t + 2], k.rearrange("a d -> d a")).then_inc(s_gain, 16)
                sp.dma_start(bf[:, :], b_forget.rearrange("a h -> h a")).then_inc(s_gain, 16)
            sp.dma_start(wf_raw, w_in[0, :, NGROUP * 4 * WG:].rearrange("(k p) c -> p k c", p=P)).then_inc(s_wf, 16)
            sp.dma_start(rel_row, rel_bias[0, :, 1:RELW]).then_inc(s_rev, 16)

            for step in PLAN:
                if step[0] == "x" and step[1] + 3 < TT:
                    t = step[1] + 3
                    if t >= XB:
                        sp.wait_ge(s_turn, 2 * (t - XB + 1))
                    load_x(t)
                if step == ("x", 4):
                    sp.wait_ge(s_revd, 2)
                    sp.dma_start(rev_d, rev_row).then_inc(s_scr, 16)
                if step[0] == "forget":
                    sp.wait_ge(s_scr, 16)
                    for h in range(HG):
                        sp.dma_start(skew_d[h], rev_d[h:h + 1, :].broadcast_to([P, REVW])).then_inc(s_skew, 16)
                    sp.wait_ge(s_fd, 4)
                    sp.dma_start(decay_d, f_rows[0]).then_inc(s_scr, 16)
                if step[0] in ("weights", "wout"):
                    load_weights(wchunk(step) + WR)
                if step[0] == "heads" and step[1] >= PPG and step[3] == 0:
                    _, j, s, _ = step
                    if j == PPG and s == 0:
                        sp.wait_ge(s_skew, 16 * HG)
                        sp.wait_ge(s_scr, 32)
                    if j > PPG:
                        sp.wait_ge(s_z, nslot((j - 1) * 2 * TT + (s + 1) * TT)[1])
                    head = 2 * (j % PPG) + s
                    if j // PPG == 1:
                        src = bass.AP(skew_d[head].tensor, head * P * REVW + P - 1, [[REVW - 1, P], [1, P * WIN]])
                        sp.dma_start(bias[:, s, 0:P * WIN], src).then_inc(s_bias[s], 16)
                    else:
                        sp.dma_start(bias[:, s, :], decay_d[head:head + 1, :].broadcast_to([P, SEQ])
                                     ).then_inc(s_bias[s], 16)
                if step[0] == "fold" and step[1] % 4 == 3:
                    n = step[1]
                    h, u = n // TT, n % TT // 4
                    sp.wait_ge(s_evac, last_turn(step))
                    sp.dma_start(mix_d[u * HALF:(u + 1) * HALF, h * HD:(h + 1) * HD].rearrange("(t p) c -> p t c", p=P),
                                 mo[:, slot(n), 4 * u:4 * u + 4, :]).then_inc(s_mo[2 * u + slot(n)], 16)
                    if n == NB - 5:
                        sp.wait_ge(s_turn, last_turn(("heads", PAIRS - 1, 1, 1)))
                        load_last(0)
                    if n == NB - 1:
                        sp.wait_ge(s_turn, turned(n))
                        load_last(1)
                if step == ("norm", PAIRS - 1, 0):
                    sp.wait_ge(s_w, 2 * TT * PPG)
                    load_first(0)
                    load_first(1)
                if step == ("mixed", 0, 0, 0):
                    for k in ((s_vlo, VGATE[PAIRS - 1, 1, 0] + 1), (s_gate, VGATE[PAIRS - 1, 1, 0] + 1),
                              (s_qn, NORM[PAIRS - 1, 0] - NORM_A + 1)):
                        sp.wait_ge(*k)
                    for i in range(4):
                        load_residual(i)
                if step[0] == "mixed" and step[1] == 0 and step[3] == 1 and step[2] + 2 < TT:
                    load_first(step[2] + 2)
                if step[0] == "part":
                    i = step[1]
                    t, c = divmod(i, 2)
                    sp.wait_ge(s_half, i + 1)
                    sp.dma_start(part_d[t * P:(t + 1) * P, c * HALF:(c + 1) * HALF],
                                 piece[i % 4]).then_inc(s_part[i % 4], 16)
                    if 1 <= i and i + 3 < 2 * TT:
                        load_residual(i + 3)
                    if i in (2 * TT - 5, 2 * TT - 1):
                        if i == 2 * TT - 5:
                            sp.wait_ge(s_vlo, VGATE[PAIRS - 1, 1, 1] + 1)
                            sp.wait_ge(s_gate, VGATE[PAIRS - 1, 1, 1] + 1)
                            sp.wait_ge(s_qn, NORM[PAIRS - 1, 1] - NORM_A + 1)
                        else:
                            sp.wait_ge(s_turn, last_turn(("mixed", 0, TT - 1, 1)))
                        for q in range(4):
                            sp.wait_ge(s_part[q], 16 * (2 if i == 2 * TT - 5 else 4))
                        u = 0 if i == 2 * TT - 5 else 2
                        load_total(u)
                        load_total(u + 1)
                if step[0] == "out":
                    t = step[1]
                    sp.wait_ge(s_res, t + 1)
                    sp.dma_start(out[0, t * P:(t + 1) * P, :], total[t % 4]).then_inc(s_out[t % 4], 16)
                    if t >= 1 and t + 3 < TT:
                        sp.wait_ge(s_out[(t - 1) % 4], 16)
                        load_total(t + 3)
            for o in s_out:
                sp.wait_ge(o, 16 * (TT // 4))

        @block.gpsimd
        def _(pool):
            nc.gpsimd.memset(ident_raw, 0.0).then_inc(s_const, 1)
            nc.gpsimd.memset(foldm[:, :], 0.0).then_inc(s_const, 1)
            nc.gpsimd.memset(bias[:, 0, 0:386], 0.0).then_inc(s_const, 1)
            nc.gpsimd.memset(mhalf[:, :], -0.5).then_inc(s_const, 1)
            nc.gpsimd.memset(rbuf[:, :, SEQ:SEQ + 1], 1.0).then_inc(s_const, 1)
            pool.wait_ge(s_const, 5)
            nc.gpsimd.affine_select(out=ident_raw, in_=ident_raw, compare_op=ALU.not_equal, fill=1.0,
                                    base=0, pattern=[[-1, P]], channel_multiplier=1).then_inc(s_const, 1)
            nc.gpsimd.affine_select(out=foldm[:, :], in_=foldm[:, :], compare_op=ALU.not_equal, fill=0.5,
                                    base=0, pattern=[[-1, HD]], channel_multiplier=1).then_inc(s_const, 1)
            nc.gpsimd.affine_select(out=bias[:, 0, 0:386], in_=bias[:, 0, 0:386], compare_op=ALU.is_gt, fill=BIG_NEG,
                                    base=129, pattern=[[-1, 386]], channel_multiplier=1).then_inc(s_const, 1)
            pool.wait_ge(s_const, 8)
            nc.gpsimd.affine_select(out=foldm[:, :], in_=foldm[:, :], compare_op=ALU.not_equal, fill=0.5,
                                    base=-HD, pattern=[[-1, HD]], channel_multiplier=1).then_inc(s_const, 1)
            for step in PLAN:
                if step[0] == "square":
                    t = step[1]
                    pool.wait_ge(s_ms, t + 1)
                    nc.gpsimd.tensor_tensor(xs[:, t % 4, 1:2], xs[:, t % 4, 0:1], mhalf[:, 0:1],
                                            ALU.pow).then_inc(s_rs, 1)
                if step[0] == "stats":
                    _, j, u = step
                    pool.wait_ge(s_ss, 2 * (j - PPG) + u + 1)
                    nc.gpsimd.tensor_tensor(rs[:, 16 * u:16 * u + 16], ms[:, 16 * u:16 * u + 16], mhalf[:, 0:16],
                                            ALU.pow).then_inc(s_rs, 1)
                if step[0] == "norm" and step[1] < PPG:
                    _, j, u = step
                    pool.wait_ge(s_raw, TT * j + 4 * u + 4)
                    if j:
                        pool.wait_ge(s_turn, last_turn(("heads", j - 1, 1, u)))
                    nc.gpsimd.tensor_copy(
                        qks[:, :, 4 * u:4 * u + 4, :, :].rearrange("p s t f c -> p t s (f c)"),
                        raw[:, 4 * u:4 * u + 4, :].rearrange("p t (s c) -> p t s c", s=2)[:, :, :, 0:P]).then_inc(s_qc, 1)
                    pool.wait_ge(s_qc, NORM[j, u] + 1)
                if step[0] == "vgate" and step[1] // PPG == 1 and step[3] == 0:
                    _, j, s, u = step
                    jj = j - PPG
                    pool.wait_ge(s_bias[s], 16 * (jj + 1))
                    nc.gpsimd.memset(bias[0:CHUNK, s, P * WIN - CHUNK:P * WIN], BIG_NEG).then_inc(s_corner, 1)
                    pool.wait_ge(s_corner, 2 * (2 * jj + s) + 1)
                    nc.gpsimd.memset(bias[CHUNK:P, s, 0:CHUNK], BIG_NEG).then_inc(s_corner, 1)
                    pool.wait_ge(s_corner, 2 * (2 * jj + s) + 2)

        @block.scalar
        def _(act):
            act.wait_ge(s_const, 9)
            nc.scalar.activation(identr[:, :], ident_raw, ACT.Copy).then_inc(s_const, 1)
            nc.scalar.activation(mask[:, :], bias[:, 0, 0:386], ACT.Copy).then_inc(s_const, 1)
            for step in PLAN:
                kind = step[0]
                if kind == "square":
                    t = step[1]
                    act.wait_ge(s_x[t % XB], 16 * (t // XB + 1))
                    if t:
                        act.wait_ge(s_xsq, t)
                    if t >= 4:
                        act.wait_ge(s_xn, t - 3)
                    nc.scalar.activation(rbuf[:, 0, 0:SEQ], xt[t % XB], ACT.Square,
                                         accum_out=xs[:, t % 4, 0:1]).then_inc(s_xsq, 1)
                if kind == "x":
                    t = step[1]
                    for u in range(2):
                        m = TURN0[step] + u
                        act.wait_ge(s_turn, m + 1)
                        nc.scalar.activation(hT[0][:, 4 * u:4 * u + 4, t * P:(t + 1) * P],
                                             psT[:, m % 2, :].rearrange("p (k q) -> p k q", k=4),
                                             ACT.Copy).then_inc(s_hi, 1)
                if kind == "forget":
                    act.wait_ge(s_wf, 16)
                    nc.scalar.activation(wf_hl[0], wf_raw, ACT.Copy).then_inc(s_fa, 1)
                    act.wait_ge(s_fd, 3)
                    nc.scalar.activation(f_rows[2], f_rows[1], ACT.Abs).then_inc(s_fa, 1)
                    act.wait_ge(s_fa, 2)
                    nc.scalar.activation(f_rows[2], f_rows[2], ACT.Exp, scale=-1.0).then_inc(s_fa, 1)
                    act.wait_ge(s_fa, 3)
                    nc.scalar.activation(f_rows[3], f_rows[2], ACT.Ln, bias=1.0).then_inc(s_fa, 1)
                if kind in ("weights", "wout"):
                    c = wchunk(step)
                    if kind == "weights":
                        dst = by_head(wpair[0][:, step[2], :])
                        src = wraw[:, c % WR, :].rearrange("p (f h c) -> p f h c", f=4, h=2)
                        if step[1]:
                            act.wait_ge(s_wk, KT * (step[1] - 1) + step[2] + 1)
                    else:
                        dst = wo[0][:, step[1] // 2, step[1] % 2 * HALF:(step[1] % 2 + 1) * HALF]
                        src = wraw[:, c % WR, :]
                        if step[1] == 0:
                            act.wait_ge(s_wk, KT * PAIRS)
                        if step[1] == 2 * MT - 4:
                            act.wait_ge(s_first, 2 * TT)
                    act.wait_ge(s_wld[c % WR], 16 * (c // WR + 1))
                    nc.scalar.activation(dst, src, ACT.Copy).then_inc(s_whi, 1)
                if kind == "raw":
                    _, j, t = step
                    i = j * TT + t
                    if t < TT - 1:
                        act.wait_ge(s_proj, j * (TT - 1) + t + 1)
                    else:
                        act.wait_ge(s_wk, KT * (j + 1))
                    if t % 4 == 0 and j:
                        act.wait_ge(s_vlo, VGATE[j - 1, 1, t // 4] + 1)
                        act.wait_ge(s_gate, VGATE[j - 1, 1, t // 4] + 1)
                        norms = NORM[j - 1, t // 4] + 1
                        if j <= PPG:
                            act.wait_ge(s_qc, norms)
                        else:
                            act.wait_ge(s_qn, norms - NORM_A)
                    nc.scalar.activation(raw[:, t, :], psP[:, :], ACT.Copy).then_inc(s_raw, 1)
                if kind == "stats":
                    _, j, u = step
                    act.wait_ge(s_turn, last_turn(("heads", j - 1, 1, u)))
                    act.wait_ge(s_raw, TT * j + 4 * u + 4)
                    nc.scalar.activation(qks[:, :, 4 * u:4 * u + 4, :, :].rearrange("p s t f c -> p t s (f c)"),
                                         raw[:, 4 * u:4 * u + 4, :].rearrange("p t (s c) -> p t s c", s=2)[:, :, :, 0:P],
                                         ACT.Square).then_inc(s_sq, 1)
                if kind == "heads":
                    _, j, s, u = step
                    g = j // PPG
                    m = TURN0[step]
                    cols = slice(u * HALF, (u + 1) * HALF)
                    last = (j - 1) * 2 * TT + (s + 1) * TT
                    if j:
                        act.wait_ge(s_scores, last)
                    else:
                        act.wait_ge(s_fd, 1)
                    act.wait_ge(s_turn, m + 1)
                    nc.scalar.activation(stack[0:HD, s, 0, cols], psT[0:HD, m % 2, :], ACT.Copy,
                                         scale=gain[0:HD, g:g + 1])
                    nc.scalar.activation(stack[0:HD, s, 1, cols], psT[HD:P, m % 2, :], ACT.Copy,
                                         scale=gain[HD:P, g:g + 1])
                    nc.scalar.activation(stack[HD:P, s, 2, cols], psT[HD:P, m % 2, :], ACT.Copy,
                                         scale=gain[HD:P, g:g + 1]).then_inc(s_hi, 1)
                if kind == "vgate":
                    _, j, s, u = step
                    last = (j - 1) * 2 * TT + (s + 1) * TT
                    if j:
                        act.wait_ge(s_pv, CHUNK0[last])
                    nc.scalar.activation(vst[:, s, 4 * u:4 * u + 4, 0:HD], part(2, s, u), ACT.Copy).then_inc(s_vhi, 1)
                    if j:
                        act.wait_ge(s_evac, last_turn(("fold", last - TT + 4 * u + 3)))
                    nc.scalar.activation(gate[:, s, 4 * u:4 * u + 4, :], part(3, s, u), ACT.Tanh,
                                         scale=0.5).then_inc(s_ge, 1)
                if kind == "scores" and group(step[1]) == 0:
                    n = step[1]
                    off, _ = score_parts(n)
                    w = window(n)[1] * P
                    src = psS[:, n % 2, off:off + w]
                    if n >= 2:
                        act.wait_ge(s_turn, turned(n - 2))
                    else:
                        act.wait_ge(s_fd, 4)
                    act.wait_ge(s_scores, n + 1)
                    nc.scalar.activation(zbuf[:, n % 2, 0:w], src, ACT.Sigmoid)
                    nc.scalar.activation(rbuf[:, n % 2, 0:w], src, ACT.Sigmoid, scale=-1.0).then_inc(s_sig, 1)
                if kind == "weigh" and group(step[1]):
                    n = step[1]
                    w = window(n)[1] * P
                    q = n % 4
                    act.wait_ge(s_nm, nslot(n)[1] + 1)
                    if n >= 4 + 2 * TT * PPG:
                        act.wait_ge(s_rd, nslot(n)[1] - 3)
                    nc.scalar.activation(zbuf[:, n % 2, 0:w], zbuf[:, n % 2, 0:w], ACT.Exp,
                                         bias=small[:, q, 1:2], accum_out=small[:, q, 2:3]).then_inc(s_exp, 1)
                if kind == "values":
                    n = step[1]
                    if n >= 2:
                        act.wait_ge(s_turn, last_turn(("fold", n - 2)))
                    act.wait_ge(s_pv, CHUNK0[n + 1])
                    nc.scalar.activation(osum[:, n % 2, :], psO[:, 0:P], ACT.Copy).then_inc(s_oc, 1)
                if kind == "turn":
                    _, n, u = step
                    nb = chunks(n)[u][1]
                    m = TURN0[step]
                    ci = CHUNK0[n] + u
                    if ci >= RING:
                        act.wait_ge(s_pv, ci - RING + 1)
                    act.wait_ge(s_turn, m + 1)
                    nc.scalar.activation(pt[:, ci % RING, 0:nb, 0, :],
                                         psT[:, m % 2, 0:nb * P].rearrange("p (b q) -> p b q", b=nb),
                                         ACT.Copy).then_inc(s_hi, 1)
                if kind == "mixed":
                    _, h, t, u = step
                    if h == 0:
                        dst = mixFT[t % 2][0][:, u * HALF:(u + 1) * HALF]
                        if t == 0:
                            act.wait_ge(s_wk, KT * PAIRS)
                        if t >= 2:
                            act.wait_ge(s_first, 2 * (t - 1))
                    else:
                        dst = mixLT[t % 2][0]
                        if t == 0:
                            act.wait_ge(s_scores, NB)
                        if t >= 2:
                            act.wait_ge(s_oacc, t - 1)
                    m = TURN0[step]
                    act.wait_ge(s_turn, m + 1)
                    nc.scalar.activation(dst, psT[:, m % 2, :], ACT.Copy).then_inc(s_hi, 1)

        @block.vector
        def _(dve):
            for step in PLAN:
                kind = step[0]
                if kind == "square":
                    t = step[1]
                    dve.wait_ge(s_xsq, t + 1)
                    nc.vector.tensor_scalar(xs[:, t % 4, 0:1], xs[:, t % 4, 0:1], 1.0 / DM, EPS, ALU.mult,
                                            ALU.add).then_inc(s_ms, 1)
                if kind == "scale":
                    t = step[1]
                    if t == 0:
                        dve.wait_ge(s_gx, 16)
                    dve.wait_ge(s_rs, t + 1)
                    nc.vector.scalar_tensor_tensor(out=xt[t % XB], in0=xt[t % XB], scalar=xs[:, t % 4, 1:2], in1=gx,
                                                   op0=ALU.mult, op1=ALU.mult).then_inc(s_xn, 1)
                if kind == "constants":
                    nc.vector.memset(gain[0:HD, 0:1], HD ** -0.5)
                    nc.vector.memset(gain[HD:P, 0:1], 1.0).then_inc(s_revd, 1)
                    dve.wait_ge(s_gain, 5 * 16)
                    dve.wait_ge(s_revd, 1)
                    nc.vector.tensor_scalar(gain[0:HD, 1:3], gain[0:HD, 1:3], HD ** -0.5, None, ALU.mult).then_inc(s_fd, 1)
                    dve.wait_ge(s_rev, 16)
                    nc.vector.tensor_copy(rev_row[:, 0:HALF], rel_row[:, RELW - 2:RELW - 1].broadcast_to([HG, HALF]))
                    nc.vector.tensor_copy(rev_row[:, HALF:HALF + RELW - 2], rel_row[:, 0:RELW - 2][:, ::-1])
                    nc.vector.memset(rev_row[:, HALF + RELW - 2:REVW], 0.0).then_inc(s_revd, 1)
                if kind == "x":
                    t = step[1]
                    for u in range(2):
                        m = TURN0[step] + u
                        dve.wait_ge(s_hi, HI0[step] + u + 1)
                        ks, q = slice(4 * u, 4 * u + 4), slice(t * P, (t + 1) * P)
                        nc.vector.tensor_tensor(hT[1][:, ks, q], psT[:, m % 2, :].rearrange("p (k q) -> p k q", k=4),
                                                hT[0][:, ks, q].bitcast(F32), ALU.subtract).then_inc(s_evac, 1)
                if kind == "forget":
                    dve.wait_ge(s_fa, 1)
                    nc.vector.tensor_tensor(wf_hl[1], wf_raw, wf_hl[0].bitcast(F32), ALU.subtract).then_inc(s_fd, 1)
                    dve.wait_ge(s_f, 1)
                    nc.vector.tensor_scalar(f_rows[1], psS[0:HG, 0, :], bf[:, 0:1], -1.0, ALU.add,
                                            ALU.mult).then_inc(s_fd, 1)
                    dve.wait_ge(s_fa, 4)
                    nc.vector.scalar_tensor_tensor(out=f_rows[2], in0=f_rows[1], scalar=0.0, in1=f_rows[3],
                                                   op0=ALU.max, op1=ALU.add).then_inc(s_sp, 1)
                    dve.wait_ge(s_sp, 1)
                    nc.vector.tensor_tensor_scan(out=f_rows[0], data0=f_rows[2], data1=f_rows[2], initial=0.0,
                                                 op0=ALU.add, op1=ALU.bypass).then_inc(s_fd, 1)
                if kind in ("weights", "wout"):
                    c = wchunk(step)
                    if kind == "weights":
                        hi, lo = (by_head(w[:, step[2], :]) for w in wpair)
                        src = wraw[:, c % WR, :].rearrange("p (f h c) -> p f h c", f=4, h=2)
                    else:
                        hi, lo = (w[:, step[1] // 2, step[1] % 2 * HALF:(step[1] % 2 + 1) * HALF] for w in wo)
                        src = wraw[:, c % WR, :]
                    dve.wait_ge(s_whi, c + 1)
                    nc.vector.tensor_tensor(lo, src, hi.bitcast(F32), ALU.subtract).then_inc(s_wlo, 1)
                if kind == "stats":
                    _, j, u = step
                    i = 2 * (j - PPG) + u
                    half = ms[:, 16 * u:16 * u + 16]
                    dve.wait_ge(s_sq, i + 1)
                    for s in range(2):
                        ins = nc.vector.tensor_reduce(half[:, 8 * s:8 * s + 8], qks[:, s, 4 * u:4 * u + 4, :, :].rearrange(
                            "p t f c -> p (t f) c"), AX.X, ALU.add)
                    ins.then_inc(s_sum, 1)
                    dve.wait_ge(s_sum, i + 1)
                    nc.vector.tensor_scalar(half, half, 1.0 / HD, EPS, ALU.mult, ALU.add).then_inc(s_ss, 1)
                if kind == "norm" and step[1] >= PPG:
                    _, j, u = step
                    dve.wait_ge(s_rs, TT + NORM[j, u] - NORM_A + 1)
                    for s in range(2):
                        r = rs[:, 16 * u + 8 * s:16 * u + 8 * s + 8].rearrange("p (t f) -> p t f", f=2)
                        for f in range(2):
                            ins = nc.vector.tensor_tensor(qks[:, s, 4 * u:4 * u + 4, f, :], part(f, s, u),
                                                          r[:, :, f:f + 1].broadcast_to([P, TT // 2, HD]), ALU.mult)
                    ins.then_inc(s_qn, 1)
                if kind == "heads":
                    _, j, s, u = step
                    g = j // PPG
                    m = TURN0[step]
                    cols = slice(u * HALF, (u + 1) * HALF)
                    dve.wait_ge(s_hi, HI0[step] + 1)
                    nc.vector.scalar_tensor_tensor(
                        out=stack[HD:P, s, 0, cols], in0=psT[0:HD, m % 2, :], scalar=gain[0:HD, g:g + 1],
                        in1=stack[0:HD, s, 0, cols].bitcast(F32), op0=ALU.mult, op1=ALU.subtract)
                    nc.vector.scalar_tensor_tensor(
                        out=stack[HD:P, s, 1, cols], in0=psT[HD:P, m % 2, :], scalar=gain[HD:P, g:g + 1],
                        in1=stack[HD:P, s, 2, cols].bitcast(F32), op0=ALU.mult, op1=ALU.subtract)
                    nc.vector.scalar_tensor_tensor(
                        out=stack[0:HD, s, 2, cols], in0=psT[HD:P, m % 2, :], scalar=gain[HD:P, g:g + 1],
                        in1=stack[HD:P, s, 2, cols].bitcast(F32), op0=ALU.mult, op1=ALU.subtract
                    ).then_inc(s_evac, 1)
                if kind == "vgate":
                    _, j, s, u = step
                    i = VGATE[j, s, u]
                    dve.wait_ge(s_vhi, i + 1)
                    nc.vector.tensor_tensor(vst[:, s, 4 * u:4 * u + 4, HD:P], part(2, s, u),
                                            vst[:, s, 4 * u:4 * u + 4, 0:HD].bitcast(F32), ALU.subtract).then_inc(s_vlo, 1)
                    gh = gate[:, s, 4 * u:4 * u + 4, :]
                    dve.wait_ge(s_ge, i + 1)
                    nc.vector.scalar_tensor_tensor(out=gh, in0=gh, scalar=1.0, in1=part(3, s, u), op0=ALU.add,
                                                   op1=ALU.mult).then_inc(s_gate, 1)
                if kind == "scores" and group(step[1]):
                    n = step[1]
                    off, _ = score_parts(n)
                    w = window(n)[1] * P
                    q = n % 4
                    i = nslot(n)[1]
                    if n % TT == 0:
                        dve.wait_ge(s_bias[slot(n)], 16 * bias_loads(n))
                        if group(n) == 1:
                            dve.wait_ge(s_corner, 2 * (n // TT - 2 * PPG + 1))
                    dve.wait_ge(s_turn, turned(n - 2))
                    dve.wait_ge(s_scores, n + 1)
                    if i >= 4:
                        dve.wait_ge(s_exp, i - 3)
                    add = bias[:, slot(n), 0:w] if group(n) == 2 else bias[:, slot(n), P * WIN - w:P * WIN]
                    nc.vector.tensor_tensor_reduce(out=zbuf[:, n % 2, 0:w], in0=psS[:, n % 2, off:off + w],
                                                   in1=add, scale=1.0, scalar=-3.0e38, op0=ALU.add, op1=ALU.max,
                                                   accum_out=small[:, q, 0:1]).then_inc(s_z, 1)
                    dve.wait_ge(s_z, i + 1)
                    nc.vector.tensor_scalar(small[:, q, 1:2], small[:, q, 0:1], -1.0, None,
                                            ALU.mult).then_inc(s_nm, 1)
                if kind == "weigh" and group(step[1]) == 0:
                    n = step[1]
                    w = window(n)[1] * P
                    dve.wait_ge(s_sig, n + 1)
                    rem = rbuf[:, n % 2, 0:w]
                    nc.vector.memset(rbuf[:, n % 2, w:w + 1], 1.0).then_inc(s_rem, 1)
                    back = rem[:, ::-1]
                    nc.vector.tensor_tensor_scan(out=back, data0=back, data1=back, initial=1.0,
                                                 op0=ALU.mult, op1=ALU.bypass).then_inc(s_rem, 1)
                    dve.wait_ge(s_rem, 2 * n + 2)
                    nc.vector.tensor_tensor(zbuf[:, n % 2, 0:w], zbuf[:, n % 2, 0:w],
                                            rbuf[:, n % 2, 1:w + 1], ALU.mult).then_inc(s_w, 1)
                if kind == "values":
                    n = step[1]
                    dve.wait_ge(s_oc, n + 1)
                    nc.vector.tensor_tensor(osum[:, n % 2, :], psO[:, P:2 * P], osum[:, n % 2, :], ALU.add).then_inc(s_os, 1)
                if kind == "turn":
                    _, n, u = step
                    nb = chunks(n)[u][1]
                    m = TURN0[step]
                    ci = CHUNK0[n] + u
                    dve.wait_ge(s_hi, HI0[step] + 1)
                    nc.vector.tensor_tensor(pt[:, ci % RING, 0:nb, 1, :],
                                            psT[:, m % 2, 0:nb * P].rearrange("p (b q) -> p b q", b=nb),
                                            pt[:, ci % RING, 0:nb, 0, :].bitcast(F32),
                                            ALU.subtract).then_inc(s_evac, 1)
                if kind == "fold":
                    n = step[1]
                    b = n % TT
                    s = slot(n)
                    m = TURN0[step]
                    if b % 4 == 0:
                        if n >= 2 * TT:
                            dve.wait_ge(s_mo[2 * (b // 4) + s], 16 * (n // (2 * TT)))
                        dve.wait_ge(s_gate, VGATE[n // (2 * TT), s, b // 4] + 1)
                    if group(n):
                        i = nslot(n)[1]
                        dve.wait_ge(s_exp, i + 1)
                        nc.vector.reciprocal(small[:, n % 4, 3:4], small[:, n % 4, 2:3]).then_inc(s_rd, 1)
                        dve.wait_ge(s_rd, i + 1)
                    dve.wait_ge(s_turn, m + 1)
                    src = psT[:, m % 2, 0:HD]
                    if group(n):
                        nc.vector.scalar_tensor_tensor(out=mo[:, s, b, :], in0=src, scalar=small[:, n % 4, 3:4],
                                                       in1=gate[:, s, b, :], op0=ALU.mult,
                                                       op1=ALU.mult).then_inc(s_evac, 1)
                    else:
                        nc.vector.tensor_tensor(mo[:, s, b, :], src, gate[:, s, b, :], ALU.mult).then_inc(s_evac, 1)
                if kind == "mixed":
                    _, h, t, u = step
                    hi, lo = (w[:, u * HALF:(u + 1) * HALF] for w in (mixFT if h == 0 else mixLT)[t % 2])
                    dve.wait_ge(s_hi, HI0[step] + 1)
                    nc.vector.tensor_tensor(lo, psT[:, TURN0[step] % 2, :], hi.bitcast(F32),
                                            ALU.subtract).then_inc(s_evac, 1)
                if kind == "part":
                    i = step[1]
                    dve.wait_ge(s_xr[i % 4], 16 * (i // 4 + 1))
                    dve.wait_ge(s_first, i + 1)
                    nc.vector.tensor_tensor(piece[i % 4], psP[:, :], piece[i % 4], ALU.add).then_inc(s_half, 1)
                if kind == "out":
                    t = step[1]
                    dve.wait_ge(s_tot[t % 4], 16 * (t // 4 + 1))
                    dve.wait_ge(s_oacc, t + 1)
                    nc.vector.tensor_tensor(total[t % 4], psS[:, t % 2, :], total[t % 4], ALU.add).then_inc(s_res, 1)

        @block.tensor
        def _(pe):
            pe.wait_ge(s_const, 11)
            for step in PLAN:
                kind = step[0]
                if kind == "x":
                    t = step[1]
                    pe.wait_ge(s_xn, t + 1)
                    for u in range(2):
                        m = TURN0[step] + u
                        if m >= 2:
                            pe.wait_ge(s_evac, m - 1)
                        for i in range(4):
                            ins = nc.tensor.transpose(psT[:, m % 2, i * P:(i + 1) * P],
                                                      xt[t % XB][:, (4 * u + i) * P:(4 * u + i + 1) * P], ident)
                        ins.then_inc(s_turn, 1)
                if kind == "forget":
                    pe.wait_ge(s_fd, 2)
                    pe.wait_ge(s_evac, 2 * TT)
                    for u in range(2):
                        for i, (a, b) in enumerate(((0, 0), (0, 1), (1, 0))):
                            for k in range(KT):
                                ins = nc.tensor.matmul(psS[0:HG, 0, u * HALF:(u + 1) * HALF], wf_hl[a][:, k, :],
                                                       hT[b][:, k, u * HALF:(u + 1) * HALF],
                                                       start=(i == 0 and k == 0), stop=(i == 2 and k == KT - 1))
                    ins.then_inc(s_f, 1)
                if kind == "project":
                    _, j, t, k0, k1 = step
                    i = j * TT + t
                    if i and k0 == 0:
                        pe.wait_ge(s_raw, i)
                    if j == 0 and k0 == 0:
                        pe.wait_ge(s_evac, last_turn(("x", t)))
                    for k in range(k0, k1):
                        if t == 0:
                            pe.wait_ge(s_wlo, KT * j + k + 1)
                        for q, (a, b) in enumerate(((0, 0), (0, 1), (1, 0))):
                            ins = nc.tensor.matmul(psP[:, :], hT[a][:, k, t * P:(t + 1) * P], wpair[b][:, k, :],
                                                   start=(k == 0 and q == 0), stop=(k == KT - 1 and q == 2))
                        if t == TT - 1:
                            ins.then_inc(s_wk, 1)
                    if k1 == KT and t < TT - 1:
                        ins.then_inc(s_proj, 1)
                if kind == "heads":
                    _, j, s, u = step
                    m = TURN0[step]
                    if j < PPG:
                        pe.wait_ge(s_qc, NORM[j, u] + 1)
                    else:
                        pe.wait_ge(s_qn, NORM[j, u] - NORM_A + 1)
                    pe.wait_ge(s_evac, m - 1)
                    for i in range(4):
                        t = 4 * u + i
                        ins = nc.tensor.transpose(psT[:, m % 2, i * P:(i + 1) * P],
                                                  qks[:, s, t, :, :].rearrange("p f c -> p (f c)"), ident)
                    ins.then_inc(s_turn, 1)
                if kind == "scores":
                    n = step[1]
                    s, b = slot(n), n % TT
                    if b % 4 == 0:
                        pe.wait_ge(s_evac, last_turn(("heads", n // (2 * TT), s, b // 4)))
                    if n >= 2:
                        a, bc = nslot(n - 1)
                        if group(n - 2):
                            pe.wait_ge(s_z, bc)
                        else:
                            pe.wait_ge(s_sig, a)
                    elif n == 0:
                        pe.wait_ge(s_fd, 3)
                    qs = stack[:, s, 0, b * P:(b + 1) * P]
                    off, parts = score_parts(n)
                    for pi, (col, key, w) in enumerate(parts):
                        dst = psS[:, n % 2, col:col + w]
                        last = pi == len(parts) - 1
                        masked = group(n) != 1 and last
                        nc.tensor.matmul(dst, qs, stack[:, s, 1, key:key + w], start=True, stop=False)
                        ins = nc.tensor.matmul(dst, qs, stack[:, s, 2, key:key + w], start=False, stop=not masked)
                        if masked:
                            end = off + P * (b + 1) if b else 256
                            m0 = (1 if b else 1 + P) - (group(n) == 2)
                            ins = nc.tensor.matmul(psS[:, n % 2, end - 256:end], identr[:, :], mask[:, m0:m0 + 256],
                                                   start=False, stop=True)
                    ins.then_inc(s_scores, 1)
                if kind == "values":
                    n = step[1]
                    s = slot(n)
                    k0, total = window(n)
                    if n % 4 == 0:
                        pe.wait_ge(s_vlo, VGATE[n // (2 * TT), s, n % TT // 4] + 1)
                    if n:
                        pe.wait_ge(s_os, n)
                    for u, (c, nb) in enumerate(chunks(n)):
                        ci = CHUNK0[n] + u
                        pe.wait_ge(s_evac, last_turn(("turn", n, u)))
                        for i in range(nb):
                            ins = nc.tensor.matmul(psO[:, 0:2 * P], vst[:, s, k0 + c + i, :],
                                                   pt[:, ci % RING, i, :, :], start=(c + i == 0),
                                                   stop=(c + i == total - 1))
                        ins.then_inc(s_pv, 1)
                if kind == "turn":
                    _, n, u = step
                    c, nb = chunks(n)[u]
                    m = TURN0[step]
                    a, bc = nslot(n + 1)
                    if group(n):
                        pe.wait_ge(s_exp, bc)
                    else:
                        pe.wait_ge(s_w, a)
                    pe.wait_ge(s_evac, m - 1)
                    for i in range(nb):
                        ins = nc.tensor.transpose(psT[:, m % 2, i * P:(i + 1) * P],
                                                  zbuf[:, n % 2, (c + i) * P:(c + i + 1) * P], ident)
                    ins.then_inc(s_turn, 1)
                if kind == "fold":
                    n = step[1]
                    m = TURN0[step]
                    pe.wait_ge(s_os, n + 1)
                    pe.wait_ge(s_evac, m - 1)
                    nc.tensor.matmul(psT[:, m % 2, 0:HD], osum[:, n % 2, :], foldm[:, :], start=True,
                                     stop=True).then_inc(s_turn, 1)
                if kind == "mixed":
                    _, h, t, u = step
                    m = TURN0[step]
                    if h == 0:
                        pe.wait_ge(s_mxf[t % 2], 16 * (t // 2 + 1))
                        src = mixF[t % 2][:, u * HALF:(u + 1) * HALF]
                    else:
                        pe.wait_ge(s_mxl[t // 4], 16)
                        src = mixL[t // 4][:, (t % 4) * HALF:(t % 4 + 1) * HALF]
                    pe.wait_ge(s_evac, m - 1)
                    for i in range(4):
                        ins = nc.tensor.transpose(psT[:, m % 2, i * P:(i + 1) * P], src[:, i * P:(i + 1) * P],
                                                  ident)
                    ins.then_inc(s_turn, 1)
                if kind == "first":
                    _, i, k0, k1 = step
                    t, c = divmod(i, 2)
                    if k0 == 0:
                        pe.wait_ge(s_evac, last_turn(("mixed", 0, t, 1)))
                        if i == 0:
                            pe.wait_ge(s_raw, TT * PAIRS)
                        else:
                            pe.wait_ge(s_half, i)
                    for k in range(k0, k1):
                        if t == 0:
                            pe.wait_ge(s_wlo, PAIRS * KT + 2 * k + c + 1)
                        for q, (a, b) in enumerate(((0, 0), (0, 1), (1, 0))):
                            ins = nc.tensor.matmul(psP[:, :], mixFT[t % 2][a][:, k * P:(k + 1) * P],
                                                   wo[b][:, k, c * HALF:(c + 1) * HALF],
                                                   start=(k == 0 and q == 0), stop=(k == MF - 1 and q == 2))
                    if k1 == MF:
                        ins.then_inc(s_first, 1)
                if kind == "out":
                    t = step[1]
                    pe.wait_ge(s_evac, last_turn(("mixed", 1, t, 0)))
                    if t == 0:
                        pe.wait_ge(s_z, NB - 2 * TT * PPG)
                    if t >= 2:
                        pe.wait_ge(s_res, t - 1)
                    for k in range(MF, MT):
                        if t == 0:
                            pe.wait_ge(s_wlo, PAIRS * KT + 2 * k + 2)
                        cols = slice((k - MF) * P, (k - MF + 1) * P)
                        for c in range(2):
                            for q, (a, b) in enumerate(((0, 0), (0, 1), (1, 0))):
                                ins = nc.tensor.matmul(psS[:, t % 2, c * HALF:(c + 1) * HALF], mixLT[t % 2][a][:, cols],
                                                       wo[b][:, k, c * HALF:(c + 1) * HALF],
                                                       start=(k == MF and q == 0), stop=(k == MT - 1 and q == 2))
                    ins.then_inc(s_oacc, 1)


_INS = ["x", "norm_g", "w_in", "b_forget", "q_norm_ch", "k_norm_ch", "q_norm_fox", "k_norm_fox", "rel_bias", "w_out"]


def kernel(**inputs):
    import numpy as _np
    import concourse.bacc as _bacc
    from concourse import mybir as _mybir
    from concourse.bass_utils import run_bass_kernel_spmd as _run

    nc = _bacc.Bacc("TRN2", target_bir_lowering=False, num_devices=1)
    arrays, args = {}, []
    for name in _INS:
        a = _np.ascontiguousarray(inputs[name])
        arrays[f"in_{name}_dram"] = a
        args.append(nc.dram_tensor(f"in_{name}_dram", a.shape, _mybir.dt.from_np(a.dtype), kind="ExternalInput").ap())
    args.append(nc.dram_tensor("out_0_dram", (1, SEQ, DM), _mybir.dt.float32, kind="ExternalOutput").ap())
    build(nc, *args)
    r = _run(nc, [arrays], core_ids=[0])
    return r.results[0]["out_0_dram"]
```
